# Optimizing a Trainium2 kernel written in Bass

```python
import jax, jax.numpy as jnp
from jax import lax
import numpy as np

D_MODEL = 1024
BATCH = 1
SEQ = 512
DEPTH = 1

CONV_WIDTH = D_MODEL // 2
CONV_K = 3
GLA_HEADS = 4
GLA_DV = (D_MODEL // 2) // GLA_HEADS
GLA_DK = GLA_DV // 2
GLA_K = GLA_HEADS * GLA_DK
GLA_V = GLA_HEADS * GLA_DV
GLA_GATE_RANK = 16
GLA_TAU = 16.0
GLA_CHUNK = 64
MIX_WIDTH = CONV_WIDTH + GLA_V
IN_COLS = 3 * CONV_WIDTH + 2 * GLA_K + 2 * GLA_V + GLA_GATE_RANK

PEER_HEADS = 8
PEER_N_KEYS = 128
PEER_N_EXPERTS = PEER_N_KEYS * PEER_N_KEYS
PEER_TOPK = 16
PEER_QDIM = 256
PEER_HALF = PEER_QDIM // 2
PEER_BLOCK = 128

LN_EPS = 1e-5
RMS_EPS = 1e-6

kernel_name = "hybrid_conv_gla_peer_deepnorm_adaln"

def _layernorm(x, g, b):
    xf = x.astype(jnp.float32)
    mu = jnp.mean(xf, axis=-1, keepdims=True)
    var = jnp.mean(jnp.square(xf - mu), axis=-1, keepdims=True)
    return ((xf - mu) * lax.rsqrt(var + LN_EPS) * g.astype(jnp.float32)
            + b.astype(jnp.float32)).astype(x.dtype)

def _short_conv_mixer(gate_b, gate_c, hval, conv_w):
    u = gate_c * hval
    seq = u.shape[1]
    up = jnp.pad(u, ((0, 0), (CONV_K - 1, 0), (0, 0)))
    z = sum(conv_w[j] * up[:, j:j + seq] for j in range(CONV_K))
    return gate_b * z

def _gla_chunked(q, k, v, g):
    bsz, seq, nh, dk = q.shape
    dv = v.shape[-1]
    nc = seq // GLA_CHUNK

    def to_chunks(a):
        return a.reshape(bsz, nc, GLA_CHUNK, nh, a.shape[-1]).transpose(0, 3, 1, 2, 4)

    q, k, v, g = (to_chunks(a.astype(jnp.float32)) for a in (q, k, v, g))
    b = jnp.cumsum(g, axis=3)
    b_last = b[:, :, :, -1:, :]
    qe = q * jnp.exp(b)
    ke = k * jnp.exp(-b)
    kl = k * jnp.exp(b_last - b)

    causal = jnp.tril(jnp.ones((GLA_CHUNK, GLA_CHUNK), dtype=bool))
    attn = jnp.einsum('bhncd,bhnmd->bhncm', qe, ke)
    attn = jnp.where(causal, attn, 0.0)
    o_intra = jnp.einsum('bhncm,bhnme->bhnce', attn, v)

    kv = jnp.einsum('bhncd,bhnce->bhnde', kl, v)
    decay = jnp.exp(b_last[:, :, :, 0, :])

    def step(state, inp):
        kv_n, dec_n = inp
        return dec_n[..., None] * state + kv_n, state

    init = jnp.zeros((bsz, nh, dk, dv), jnp.float32)
    _, s_prev = lax.scan(step, init, (jnp.moveaxis(kv, 2, 0), jnp.moveaxis(decay, 2, 0)))
    s_prev = jnp.moveaxis(s_prev, 0, 2)
    o_inter = jnp.einsum('bhncd,bhnde->bhnce', qe, s_prev)

    o = o_intra + o_inter
    return o.transpose(0, 2, 3, 1, 4).reshape(bsz, seq, nh, dv)

def _peer(h, peer_wq, peer_subkeys, peer_u, peer_v):
    bsz, seq, dm = h.shape
    ntok = bsz * seq
    t = h.reshape(ntok, dm)
    q = (t @ peer_wq).reshape(ntok, PEER_HEADS, 2, PEER_HALF)
    s = jnp.einsum('thpd,hpnd->thpn', q.astype(jnp.float32), peer_subkeys.astype(jnp.float32))
    s1, i1 = lax.top_k(s[:, :, 0], PEER_TOPK)
    s2, i2 = lax.top_k(s[:, :, 1], PEER_TOPK)
    cand = (s1[..., :, None] + s2[..., None, :]).reshape(ntok, PEER_HEADS, PEER_TOPK * PEER_TOPK)
    cidx = (i1[..., :, None] * PEER_N_KEYS + i2[..., None, :]).reshape(ntok, PEER_HEADS, PEER_TOPK * PEER_TOPK)
    top, pos = lax.top_k(cand, PEER_TOPK)
    idx = jnp.take_along_axis(cidx, pos, axis=-1)
    gate = jax.nn.softmax(top, axis=-1).astype(h.dtype)

    nb = ntok // PEER_BLOCK

    def block(args):
        tb, ib, gb = args
        u = peer_u[ib]
        a = jax.nn.gelu(jnp.einsum('thkd,td->thk', u, tb), approximate=False)
        vv = peer_v[ib]
        return jnp.einsum('thk,thkd->td', gb * a, vv)

    out = lax.map(block, (t.reshape(nb, PEER_BLOCK, dm),
                          idx.reshape(nb, PEER_BLOCK, PEER_HEADS, PEER_TOPK),
                          gate.reshape(nb, PEER_BLOCK, PEER_HEADS, PEER_TOPK)))
    return out.reshape(bsz, seq, dm)

def setup_inputs(seed: int = 0) -> dict:
    key = jax.random.key(seed)
    ks = jax.random.split(key, 20)
    beta = (8.0 * DEPTH) ** -0.25
    f32 = jnp.float32
    nrm = lambda k, shape, s: (jax.random.normal(k, shape, f32) * s)
    return {
        "x": nrm(ks[0], (BATCH, SEQ, D_MODEL), 1.0),
        "c": nrm(ks[1], (BATCH, D_MODEL), 1.0),
        "w_mod": nrm(ks[2], (D_MODEL, 6 * D_MODEL), 0.5 * D_MODEL ** -0.5),
        "b_mod": nrm(ks[3], (6 * D_MODEL,), 0.02),
        "w_in": nrm(ks[4], (D_MODEL, IN_COLS), D_MODEL ** -0.5),
        "conv_w": nrm(ks[5], (CONV_K, CONV_WIDTH), CONV_K ** -0.5),
        "gla_gate_up": nrm(ks[6], (GLA_GATE_RANK, GLA_K), GLA_GATE_RANK ** -0.5),
        "gla_gate_bias": nrm(ks[7], (GLA_K,), 0.1),
        "gla_norm_g": 1.0 + nrm(ks[8], (GLA_V,), 0.02),
        "w_out": nrm(ks[9], (MIX_WIDTH, D_MODEL), beta * MIX_WIDTH ** -0.5),
        "ln1_g": 1.0 + nrm(ks[10], (D_MODEL,), 0.02),
        "ln1_b": nrm(ks[11], (D_MODEL,), 0.02),
        "peer_wq": nrm(ks[12], (D_MODEL, PEER_HEADS * PEER_QDIM), D_MODEL ** -0.5),
        "peer_subkeys": nrm(ks[13], (PEER_HEADS, 2, PEER_N_KEYS, PEER_HALF), PEER_HALF ** -0.5),
        "peer_u": nrm(ks[14], (PEER_N_EXPERTS, D_MODEL), D_MODEL ** -0.5),
        "peer_v": nrm(ks[15], (PEER_N_EXPERTS, D_MODEL), beta),
        "ln2_g": 1.0 + nrm(ks[16], (D_MODEL,), 0.02),
        "ln2_b": nrm(ks[17], (D_MODEL,), 0.02),
    }

def reference(x, c, w_mod, b_mod, w_in, conv_w, gla_gate_up, gla_gate_bias, gla_norm_g,
              w_out, ln1_g, ln1_b, peer_wq, peer_subkeys, peer_u, peer_v, ln2_g, ln2_b):
    alpha = (2.0 * DEPTH) ** 0.25
    bsz, seq, _ = x.shape
    for _layer in range(DEPTH):
        mod = jax.nn.silu(c) @ w_mod + b_mod
        shift1, scale1, gate1, shift2, scale2, gate2 = (m[:, None, :] for m in jnp.split(mod, 6, axis=-1))

        h = x * (1.0 + scale1) + shift1
        proj = h @ w_in
        offs = np.cumsum([CONV_WIDTH, CONV_WIDTH, CONV_WIDTH, GLA_K, GLA_K, GLA_V, GLA_V]).tolist()
        cb, cc, ch, q, k, v, r, glr = jnp.split(proj, offs, axis=-1)

        y_conv = _short_conv_mixer(cb, cc, ch, conv_w)

        log_a = jax.nn.log_sigmoid((glr @ gla_gate_up + gla_gate_bias).astype(jnp.float32)) / GLA_TAU
        o = _gla_chunked(q.reshape(bsz, seq, GLA_HEADS, GLA_DK) * (GLA_DK ** -0.5),
                         k.reshape(bsz, seq, GLA_HEADS, GLA_DK),
                         v.reshape(bsz, seq, GLA_HEADS, GLA_DV),
                         log_a.reshape(bsz, seq, GLA_HEADS, GLA_DK))
        o = o * lax.rsqrt(jnp.mean(jnp.square(o), axis=-1, keepdims=True) + RMS_EPS)
        o = o.reshape(bsz, seq, GLA_V) * gla_norm_g.astype(jnp.float32)
        y_gla = (o * jax.nn.silu(r.astype(jnp.float32))).astype(x.dtype)

        y_mix = jnp.concatenate([y_conv, y_gla], axis=-1) @ w_out
        x = _layernorm(alpha * x + (1.0 + gate1) * y_mix, ln1_g, ln1_b)

        h2 = x * (1.0 + scale2) + shift2
        y_ffn = _peer(h2, peer_wq, peer_subkeys, peer_u, peer_v)
        x = _layernorm(alpha * x + (1.0 + gate2) * y_ffn, ln2_g, ln2_b)
    return x


_drawn_inputs = setup_inputs


def setup_inputs(seed=0):
    import zlib

    import numpy as np

    out = dict(_drawn_inputs(seed))
    spreads = {}
    factors = {'gla_norm_g': 3.039, 'ln2_g': 2.868, 'ln2_b': 2.874}
    for name, (base, spread) in spreads.items():
        noise = np.random.default_rng([zlib.crc32(name.encode()), seed]).standard_normal(out[name].shape)
        drawn = base * np.exp(spread * noise) if base else spread * noise
        out[name] = __import__('jax').numpy.asarray(drawn.astype(out[name].dtype))
    for name, factor in factors.items():
        out[name] = (out[name] * factor).astype(out[name].dtype)
    return out
```

```python
from contextlib import ExitStack

import concourse.bass as bass
from concourse import mybir

F32 = mybir.dt.float32
U32 = mybir.dt.uint32
ALU = mybir.AluOpType
ACT = mybir.ActivationFunctionType

P = 128
LN_EPS = 1e-5
RMS_EPS = 1e-6
GLA_TAU = 16.0
CHUNK = 64
TOPK = 16
RING = 8
STEP = 4
LOWEST = -3.0e38


def build(nc, x, c, w_mod, b_mod, w_in, conv_w, gla_gate_up, gla_gate_bias, gla_norm_g, w_out,
          ln1_g, ln1_b, peer_wq, peer_subkeys, peer_u, peer_v, ln2_g, ln2_b, out):
    _, SEQ, D = x.shape
    KC = D // P
    NB = SEQ // P
    CW = conv_w.shape[1]
    CC = CW // P
    RANK, GK = gla_gate_up.shape
    GV = gla_norm_g.shape[0]
    GH = GV // P
    GP = GK // P
    DK = GK // GH
    NCH = SEQ // CHUNK
    HEADS, _, NKEYS, HALF = peer_subkeys.shape
    QD = 2 * HALF
    NG = HEADS * NB
    ALPHA = 2.0 ** 0.25
    assert NB == 4 and HALF == P and NKEYS == P

    ctx = ExitStack()
    with ctx:
        def sb(name, shape, dt=F32):
            return ctx.enter_context(nc.sbuf_tensor(name, shape, dt))

        def psum(name):
            return ctx.enter_context(nc.psum_tensor(name, [P, 1024], F32))

        def sem(name):
            return ctx.enter_context(nc.semaphore(name))

        u_ring = sb("u_ring", [P, RING, D])
        v_ring = sb("v_ring", [P, RING, D])
        x_sb = sb("x_sb", [P, NB, D])
        hT = sb("hT", [P, KC, SEQ])
        h2 = sb("h2", [P, NB, D])
        mixT = sb("mixT", [P, KC, SEQ])
        rows = sb("rows", [P, 6 * D])
        mid = sb("mid", [P, 6656])
        gx = sb("gx", [P, 3 * 1024])
        wq_sb = sb("wq_sb", [P, KC, QD])
        sk_sb = sb("sk_sb", [P, 2, HALF])
        skT = sb("skT", [P, 2, NKEYS])
        ident = sb("ident", [P, P])
        ones = sb("ones", [P, P])
        causal = sb("causal", [P, P])
        restart = sb("restart", [P, SEQ])
        prow = sb("prow", [32, P])
        pcol = sb("pcol", [P, 32])
        siluc = sb("siluc", [P, KC])
        modc = sb("modc", [P, 2 * KC])
        gate_up = sb("gate_up", [RANK, GK])

        w_ring = u_ring[:, :, :].rearrange("p a b -> p (a b)").rearrange("p (s k c) -> p s k c", s=4, k=KC)
        m_ring = v_ring[:, :, :].rearrange("p a b -> p (a b)").rearrange("p (s c) -> p s c", s=4)
        wout = v_ring
        h2f = h2[:, :, :].rearrange("p a b -> p (a b)")
        cgate = h2f[:, 0:CC * SEQ].rearrange("p (c t) -> p c t", c=CC)
        uconv = h2f[:, CC * SEQ:2 * CC * SEQ].rearrange("p (c t) -> p c t", c=CC)
        q_ = mid[:, 0:1024].rearrange("p (c t) -> p c t", c=GP)
        k_ = mid[:, 1024:2048].rearrange("p (c t) -> p c t", c=GP)
        v_ = mid[:, 2048:4096].rearrange("p (b e) -> p b e", b=NB)
        r_ = mid[:, 4096:6144].rearrange("p (h t) -> p h t", h=GH)
        glr = mid[0:RANK, 6144:6656]
        gx0, gx1, gx2 = (gx[:, 1024 * i:1024 * (i + 1)] for i in range(3))
        uf = u_ring[:, :, :].rearrange("p a b -> p (a b)")
        klT = uf[:, 0:1024].rearrange("p (c b d) -> p c b d", c=GP, b=NB)
        state = uf[:, 1024:1024 + GP * (NCH - 1) * P].rearrange("p (c n e) -> p c n e", c=GP, n=NCH - 1)
        attn = uf[:, 3072:4096].rearrange("p (i b t) -> p i b t", i=2, b=NB)
        sq = uf[:, 4096:5120].rearrange("p (i t) -> p i t", i=2)
        rms = uf[:, 5120:6144].rearrange("p (i t) -> p i t", i=2)

        diag = mid[:, 0:2048].rearrange("p (s t) -> p s t", s=TOPK)
        ln_t = mid[:, 2048:3072]
        ln_o = mid[:, 3072:4096]
        qT = mid[:, 4096:5120].rearrange("p (a t) -> p a t", a=2)
        yacc = mixT[:, :, :].rearrange("p a b -> p (a b)").rearrange("p (b d) -> p b d", b=NB)
        at = [0]

        def small(shape, dt=F32):
            n = 1
            for s in shape:
                n *= s
            v = gx[:, at[0]:at[0] + n]
            at[0] += n
            if dt is not F32:
                v = v.bitcast(dt)
            if len(shape) == 2:
                v = v.rearrange("p (a b) -> p a b", a=shape[0])
            if len(shape) == 3:
                v = v.rearrange("p (a b c) -> p a b c", a=shape[0], b=shape[1])
            return v

        rest = small([2, NKEYS])
        best = small([2, TOPK])
        besti = small([2, TOPK], U32)
        bestf = small([2, TOPK])
        cand = small([TOPK, TOPK])
        cand2 = small([TOPK, TOPK])
        pos = small([TOPK], U32)
        part = small([TOPK, 2], U32)
        partf = small([TOPK, 2])
        pick = small([TOPK, 2, TOPK])
        keys = small([TOPK, 2])
        top = small([2, TOPK])
        ntop = small([2, 1])
        expo = small([2, TOPK])
        esum = small([2, 1])
        rsum = small([1])
        dots = small([2, TOPK])
        act_ = small([2, TOPK])
        coef = small([2, TOPK])
        stats = small([2, 6])
        mv = small([2])
        std = small([1])
        rstd = small([1])
        seq16 = sb("seq16", [P, TOPK])
        idx = sb("idx", [P, NB, TOPK], U32)

        mod_cols = rows[:, 0:2 * D]
        lng, lnb = rows[:, 0:D], rows[:, D:2 * D]
        gate1, shift2, scale2, gate2 = (rows[:, D * i:D * (i + 1)] for i in (2, 3, 4, 5))

        pa, pb, pc, pd = psum("pa"), psum("pb"), psum("pc"), psum("pd")
        bank = [t[:, 512 * i:512 * (i + 1)] for t in (pa, pb, pc, pd) for i in range(2)]
        yps = [pa, pb]
        sps = [pd[:, 512 * i:512 * i + 256].rearrange("p (a n) -> p a n", a=2) for i in range(2)]

        s_par = sem("params_landed")
        s_bmod = sem("b_mod_landed")
        s_x = sem("x_landed")
        s_m = [sem(f"w_mod_landed{i}") for i in range(4)]
        s_w = [sem(f"w_in_landed{i}") for i in range(4)]
        s_lnr = sem("ln_rows_landed")
        s_ln2r = sem("ln2_rows_landed")
        s_wo = sem("w_out_landed")
        s_wq = sem("wq_landed")
        s_u = [sem(f"u_landed{i}") for i in range(RING)]
        s_v = [sem(f"v_landed{i}") for i in range(RING)]
        s_out = sem("out_stored")
        s_const = sem("constants_made")
        s_zero = sem("rows_zeroed")
        s_colps = sem("param_columns_in_psum")
        s_col = sem("param_columns_ready")
        s_xt = sem("x_transposed")
        s_xte = sem("x_transposes_copied")
        s_mu = sem("w_mod_tile_used")
        s_mc = sem("mod_columns_in_psum")
        s_mce = sem("mod_columns_ready")
        s_h = sem("hT_ready")
        s_job = sem("projection_in_psum")
        s_ja = sem("projection_copied_by_scalar")
        s_jv = sem("projection_read_by_vector")
        s_rb = sem("mod_rows_in_psum")
        s_rbe = sem("mod_rows_ready")
        s_z = sem("gate_in_psum")
        s_gs = sem("gate_step_of_scalar")
        s_gv = sem("gate_step_of_vector")
        s_klp = sem("klT_in_psum")
        s_klt = sem("klT_ready")
        s_kv = sem("kv_in_psum")
        s_st = sem("state_ready")
        s_at = sem("scores_of_attention_in_psum")
        s_am = sem("attention_masked")
        s_o = sem("o_in_psum")
        s_sq = sem("o_squared")
        s_ms = sem("mean_square_in_psum")
        s_msv = sem("mean_square_read")
        s_rt = sem("rms_root_ready")
        s_mix = sem("mix_ready")
        s_wop = sem("w_out_product_in_psum")
        s_lv = sem("ln_variance_ready")
        s_ls = sem("ln_std_ready")
        s_lnz = sem("w_out_product_read")
        s_h2 = sem("h2_ready")
        s_tp = sem("h2_transposed")
        s_tpe = sem("h2T_ready")
        s_skp = sem("subkeys_transposed")
        s_ske = sem("subkeysT_ready")
        s_qp = sem("query_in_psum")
        s_qe = sem("query_ready")
        s_sc = sem("scores_in_psum")
        s_scr = sem("scores_read")
        s_top = sem("top_ready")
        s_exp = sem("exp_ready")
        s_idx = sem("idx_ready")
        s_dot = sem("dot_done")
        s_gel = sem("gelu_ready")
        s_coef = sem("coef_ready")
        s_diag = sem("diag_ready")
        s_vu = sem("v_rows_used")
        s_yr = sem("y_read")
        s_fin = sem("result_ready")

        WT = 256
        tiles = [12, 6, 7, 8, 9, 10, 11, 2, 4, 0, 3, 5, 1]
        q_tile, k_tile, v_tile, r_tile, g_tile = 6, 7, 8, 10, 12
        jobs = []
        for n, t in enumerate(tiles):
            if t == g_tile:
                jobs.append((n, "glr", 0))
            elif t == q_tile or t == k_tile:
                jobs += [(n, "q" if t == q_tile else "k", i) for i in range(2)]
            elif v_tile <= t < v_tile + 2:
                jobs += [(n, "v", (t - v_tile, i)) for i in range(2)]
            elif r_tile <= t < r_tile + 2:
                jobs += [(n, "r", 2 * (t - r_tile) + i) for i in range(2)]
            else:
                kind = ("cb", "cc", "ch")[t // 2]
                jobs += [(n, kind, 2 * (t % 2) + i) for i in range(2)]
        by_vector = ("cb", "ch")
        read_by, counts = [], {"a": 0, "v": 0}
        for _, kind, _ in jobs:
            e = "v" if kind in by_vector else "a"
            counts[e] += 1
            read_by.append((e, counts[e]))
        first_job = [min(j for j, job in enumerate(jobs) if job[0] == n) for n in range(len(tiles))]
        last_job = [max(j for j, job in enumerate(jobs) if job[0] == n) for n in range(len(tiles))]
        MT = 3 * KC

        def mod_tile(i):
            return (i, 0) if i < KC else ((i - KC) // 2, 2 * D * (1 + (i - KC) % 2))

        block = ctx.enter_context(nc.Block())

        @block.sync
        def _(sp):
            sp.dma_start(prow[0:8, :], c.rearrange("a (k p) -> (a k) p", p=P)).then_inc(s_par, 16)
            sp.dma_start(prow[8:10, :], gla_gate_bias.rearrange("(k p) -> k p", p=P)).then_inc(s_par, 16)
            sp.dma_start(prow[10:14, :], gla_norm_g.rearrange("(k p) -> k p", p=P)).then_inc(s_par, 16)
            sp.dma_start(prow[14:26, :], conv_w.rearrange("j (k p) -> (j k) p", p=P)).then_inc(s_par, 16)
            sp.wait_ge(s_zero, 1)
            sp.dma_start(rows[0:1, :], b_mod.rearrange("(a n) -> a n", a=1)).then_inc(s_bmod, 16)

            def load_mod(i):
                k, col = mod_tile(i)
                if i >= 4:
                    sp.wait_ge(s_mu, i - 3)
                sp.dma_start(m_ring[:, i % 4, :], w_mod[k * P:(k + 1) * P, col:col + 2 * D]).then_inc(s_m[i % 4], 16)

            def load_win(n):
                if n >= 4:
                    sp.wait_ge(s_job, last_job[n - 4] + 1)
                col = WT * tiles[n]
                width = min(WT, w_in.shape[1] - col)
                sp.dma_start(w_ring[:, n % 4, :, 0:width],
                             w_in[:, col:col + width].rearrange("(k p) c -> p k c", p=P)).then_inc(s_w[n % 4], 16)

            for i in range(4):
                load_mod(i)
            sp.dma_start(x_sb[:, :, :], x[0].rearrange("(b p) d -> p b d", p=P)).then_inc(s_x, 16)
            for i in range(4, KC):
                load_mod(i)
            sp.dma_start(gate_up[:, :], gla_gate_up).then_inc(s_wq, 16)
            for n in range(4):
                load_win(n)
            i = KC
            for n in range(4, len(tiles)):
                for _ in range(6 if n == 4 else 4):
                    if i < MT:
                        load_mod(i)
                        i += 1
                load_win(n)
                if n == 5:
                    sp.dma_start(wq_sb[:, :, :], peer_wq[:, 0:QD].rearrange("(k p) c -> p k c", p=P)).then_inc(s_wq, 16)
                    sp.dma_start(sk_sb[:, :, :], peer_subkeys[0].rearrange("a n d -> n a d")).then_inc(s_wq, 16)
                if n == 7:
                    sp.wait_ge(s_mce, 1)
                    sp.dma_start(lng, ln1_g.partition_broadcast(P)).then_inc(s_lnr, 16)
                    sp.dma_start(lnb, ln1_b.partition_broadcast(P)).then_inc(s_lnr, 16)
                if n == 9:
                    sp.wait_ge(s_mu, MT)
                    sp.dma_start(wout[:, :, :], w_out.rearrange("(k p) n -> p k n", p=P)).then_inc(s_wo, 16)
            sp.wait_ge(s_h2, NB)
            sp.dma_start(lng, ln2_g.partition_broadcast(P)).then_inc(s_ln2r, 16)
            sp.dma_start(lnb, ln2_b.partition_broadcast(P)).then_inc(s_ln2r, 16)
            with sp.Fori(1, HEADS) as h:
                sp.wait_ge(s_qp, NB + h - 1)
                sp.dma_start(wq_sb[:, :, :], peer_wq[:, bass.ds(h * QD, QD)].rearrange("(k p) c -> p k c", p=P)).then_inc(s_wq, 16)
                sp.dma_start(sk_sb[:, :, :], peer_subkeys[bass.ds(h, 1)].rearrange("o a n d -> n (o a) d")).then_inc(s_wq, 16)
            for b in range(NB):
                sp.wait_ge(s_fin, b + 1)
                sp.dma_start(out[0, b * P:(b + 1) * P, :], x_sb[:, b, :]).then_inc(s_out, 16)
            sp.wait_ge(s_out, 16 * NB)

        @block.gpsimd
        def _(pool):
            nc.gpsimd.memset(rows[:, :], 0.0).then_inc(s_zero, 1)
            nc.gpsimd.memset(ident[:, :], 0.0)
            nc.gpsimd.memset(ones[:, :], 1.0)
            nc.gpsimd.memset(causal[:, :], 1.0)
            nc.gpsimd.memset(restart[:, :], 1.0)
            nc.gpsimd.iota(seq16[:, :], [[1, TOPK]], base=0, channel_multiplier=0,
                           allow_small_or_imprecise_dtypes=True)
            pool.drain()
            nc.gpsimd.affine_select(out=ident[:, :], in_=ident[:, :], compare_op=ALU.not_equal, fill=1.0,
                                    base=0, pattern=[[-1, P]], channel_multiplier=1)
            nc.gpsimd.affine_select(out=causal[:, :], in_=causal[:, :], compare_op=ALU.is_ge, fill=0.0,
                                    base=0, pattern=[[1, P]], channel_multiplier=-1)
            nc.gpsimd.memset(restart[:, :].rearrange("p (n t) -> p n t", t=CHUNK)[:, :, 0:1], 0.0)
            pool.drain()
            nc.gpsimd.memset(causal[0:CHUNK, CHUNK:P], 0.0).then_inc(s_const, 1)

            def gather(ring, table, idx_col, landed):
                pool.indirect_dma_start(ring, None, table[:, :],
                                        bass.IndirectOffsetOnAxis(ap=idx_col, axis=0)).then_inc(landed, 16)

            def slot(h, b, g, u=True, v=True):
                first = isinstance(g, int) and g < 2
                if u:
                    pool.wait_ge(s_idx, g + 1)
                    pool.nop(nofuse=True)
                for s in range(TOPK):
                    if u and s % STEP == 0 and not (g is 0 and s < RING):
                        pool.wait_ge(s_dot, 16 * g + s + STEP - RING)
                        pool.nop(nofuse=True)
                    if u:
                        gather(u_ring[:, s % RING, :], peer_u, idx[:, b, s:s + 1], s_u[s % RING])
                    if v and s == 0 and first:
                        pool.wait_ge(s_wop, NB)
                        pool.nop(nofuse=True)
                    if v and s % STEP == 0 and not (first and s < RING):
                        pool.wait_ge(s_vu, 16 * (g - 1) + s + STEP - RING)
                        pool.nop(nofuse=True)
                    if v:
                        gather(v_ring[:, s % RING, :], peer_v, idx[:, (b - 1) % NB, s:s + 1], s_v[s % RING])

            for b in range(NB):
                slot(0, b, b, v=b > 0)
            with pool.Fori(1, HEADS) as h:
                for b in range(NB):
                    slot(h, b, h * NB + b)
            slot(HEADS, 0, NG, u=False)

        @block.scalar
        def _(act):
            def copy(dst, src):
                return nc.scalar.activation(dst, src, ACT.Copy)

            act.wait_ge(s_colps, 1)
            copy(pcol[:, 0:26], bank[6][:, 0:26])
            act.drain()
            nc.scalar.activation(siluc[:, :], pcol[:, 0:KC], ACT.Silu).then_inc(s_col, 1)
            for k in range(KC):
                act.wait_ge(s_xt, k + 1)
                copy(hT[:, k, :], bank[4 + k % 2]).then_inc(s_xte, 1)
            act.wait_ge(s_mc, 1)
            copy(modc[:, 0:KC], bank[7][:, 0:KC])
            nc.scalar.activation(modc[:, KC:2 * KC], bank[7][:, KC:2 * KC], ACT.Identity, bias=1.0).then_inc(s_mce, 1)
            act.drain()
            for k in range(KC):
                nc.scalar.activation(hT[:, k, :], hT[:, k, :], ACT.Identity, bias=modc[:, k:k + 1],
                                     scale=modc[:, KC + k:KC + k + 1]).then_inc(s_h, 1)

            def mod_rows():
                for j in range(8):
                    act.wait_ge(s_rb, j + 1)
                    plus = 0.0 if j // 2 == 1 else 1.0
                    nc.scalar.activation(rows[:, 2 * D + 512 * j:2 * D + 512 * (j + 1)], bank[6 + j % 2],
                                         ACT.Identity, bias=plus).then_inc(s_rbe, 1)

            def gate_chain():
                zz = gx0.rearrange("p (c t) -> p c t", c=GP)
                for i in range(GP):
                    act.wait_ge(s_z, i + 1)
                    nc.scalar.activation(zz[:, i, :], bank[4 + i], ACT.Identity,
                                         bias=pcol[:, 8 + i:9 + i]).then_inc(s_gs, 1)
                act.drain()
                nc.scalar.activation(gx1, gx0, ACT.Abs)
                act.drain()
                nc.scalar.activation(gx1, gx1, ACT.Exp, scale=-1.0)
                act.drain()
                nc.scalar.activation(gx1, gx1, ACT.Ln, bias=1.0).then_inc(s_gs, 1)
                act.wait_ge(s_gv, 1)
                nc.scalar.activation(gx0, gx1, ACT.Exp, scale=1.0 / GLA_TAU).then_inc(s_gs, 1)
                act.wait_ge(s_gv, 2)
                nc.scalar.activation(gx2, gx2, ACT.Exp, scale=1.0 / GLA_TAU).then_inc(s_gs, 1)
                nc.scalar.activation(gx1, gx1, ACT.Exp, scale=-1.0 / GLA_TAU).then_inc(s_gs, 1)

            for j, (n, kind, i) in enumerate(jobs):
                if kind in by_vector:
                    continue
                act.wait_ge(s_job, j + 1)
                src = bank[j % 4]
                if kind == "glr":
                    copy(glr, src[0:RANK, :]).then_inc(s_ja, 1)
                elif kind == "q":
                    copy(q_[:, i, :], src).then_inc(s_ja, 1)
                elif kind == "k":
                    copy(k_[:, i, :], src).then_inc(s_ja, 1)
                elif kind == "v":
                    copy(v_[:, 2 * i[1]:2 * i[1] + 2, WT * i[0]:WT * (i[0] + 1)],
                         src.rearrange("p (b e) -> p b e", b=2)).then_inc(s_ja, 1)
                elif kind == "r":
                    nc.scalar.activation(r_[:, i, :], src, ACT.Silu).then_inc(s_ja, 1)
                else:
                    copy(cgate[:, i, :], src).then_inc(s_ja, 1)
                if kind == "r" and i == 3:
                    mod_rows()
                    gate_chain()

            for i in range(GP):
                act.wait_ge(s_klp, i + 1)
                copy(klT[:, i].rearrange("p b d -> p (b d)"), bank[4 + i]).then_inc(s_klt, 1)
            for hd in range(GH):
                act.wait_ge(s_o, hd + 1)
                nc.scalar.activation(sq[:, hd % 2, :], bank[4 + hd % 2], ACT.Square).then_inc(s_sq, 1)
                if hd >= 1:
                    act.wait_ge(s_msv, hd)
                    nc.scalar.activation(rms[:, (hd - 1) % 2, :], rms[:, (hd - 1) % 2, :], ACT.Sqrt).then_inc(s_rt, 1)
            act.wait_ge(s_msv, GH)
            nc.scalar.activation(rms[:, (GH - 1) % 2, :], rms[:, (GH - 1) % 2, :], ACT.Sqrt).then_inc(s_rt, 1)

            def ln_root(n):
                act.wait_ge(s_lv, n)
                nc.scalar.activation(std, mv[:, 1:2], ACT.Sqrt).then_inc(s_ls, 1)

            def copy_subkeys(h):
                act.wait_ge(s_skp, h + 1)
                copy(skT[:, :, :].rearrange("p a n -> p (a n)"), pc[:, 0:2 * NKEYS]).then_inc(s_ske, 1)

            def front(b):
                ln_root(b + 1)
                if b == 0:
                    copy_subkeys(0)
                for half in range(2):
                    act.wait_ge(s_tp, 2 * b + half + 1)
                    copy(hT[:, 4 * half:4 * half + 4, b * P:(b + 1) * P],
                         bank[4 + half].rearrange("p (k t) -> p k t", k=4)).then_inc(s_tpe, 1)
                act.wait_ge(s_qp, b + 1)
                copy(qT[:, :, b * P:(b + 1) * P],
                     pc[:, :].rearrange("p (a t) -> p a t", a=2)[:, :, 0:P]).then_inc(s_qe, 1)

            def softmax_top(g, par):
                act.wait_ge(s_top, g + 1)
                nc.scalar.activation(expo[:, par, :], top[:, par, :], ACT.Exp, bias=ntop[:, par, :],
                                     accum_out=esum[:, par, :]).then_inc(s_exp, 1)

            def slot(h, b, g, more=True, first=False):
                if more:
                    softmax_top(g + 1, (b + 1) % 2)
                if first:
                    front(2)
                    front(3)
                act.wait_ge(s_dot, 16 * g + 16)
                nc.scalar.activation(act_[:, b % 2, :], dots[:, b % 2, :], ACT.Gelu).then_inc(s_gel, 1)
                act.wait_ge(s_coef, g + 1)
                for s in range(TOPK):
                    if not first:
                        act.wait_ge(s_vu, 16 * (g - 1) + s + 1)
                    nc.scalar.activation(diag[:, s, :], ident[:, :], ACT.Copy,
                                         scale=coef[:, b % 2, s:s + 1]).then_inc(s_diag, 1)

            def next_head(h):
                copy_subkeys(h)
                act.wait_ge(s_qp, NB + h)
                copy(qT[:, :, :].rearrange("p a t -> p (a t)"), pc[:, :]).then_inc(s_qe, 1)

            front(0)
            softmax_top(0, 0)
            front(1)
            for b in range(NB):
                slot(0, b, b, first=b == 0)
                if b == 1:
                    next_head(1)
            with act.Fori(1, HEADS - 1) as h:
                for b in range(NB):
                    slot(h, b, h * NB + b)
                    if b == 1:
                        next_head(h + 1)
            for b in range(NB):
                slot(HEADS - 1, b, NG - NB + b, more=b < NB - 1)
                if b > 0:
                    ln_root(NB + b)
            ln_root(2 * NB)

        @block.vector
        def _(dve):
            dve.wait_ge(s_col, 1)
            dve.wait_ge(s_bmod, 16)
            for i in range(MT):
                k, col = mod_tile(i)
                dve.wait_ge(s_m[i % 4], 16 * (i // 4 + 1))
                acc = rows[:, col:col + 2 * D]
                nc.vector.scalar_tensor_tensor(out=acc, in0=m_ring[:, i % 4, :], scalar=siluc[:, k:k + 1],
                                               in1=acc, op0=ALU.mult, op1=ALU.add).then_inc(s_mu, 1)
                dve.drain()

            dve.wait_ge(s_gs, GP + 1)
            nc.vector.scalar_tensor_tensor(out=gx0, in0=gx0, scalar=0.0, in1=gx1, op0=ALU.min, op1=ALU.subtract)
            dve.drain()
            for i in range(GP):
                last = nc.vector.tensor_tensor_scan(gx1[:, SEQ * i:SEQ * (i + 1)], restart[:, :],
                                                    gx0[:, SEQ * i:SEQ * (i + 1)], 0.0, ALU.mult, ALU.add)
            last.then_inc(s_gv, 1)
            dve.drain()
            bch = gx1.rearrange("p (n t) -> p n t", t=CHUNK)
            nc.vector.tensor_tensor(gx2.rearrange("p (n t) -> p n t", t=CHUNK),
                                    bch[:, :, CHUNK - 1:CHUNK].to_broadcast((P, GP * NCH, CHUNK)),
                                    bch, ALU.subtract).then_inc(s_gv, 1)
            dve.wait_ge(s_gs, GP + 2)
            qf, kf = mid[:, 0:1024], mid[:, 1024:2048]
            nc.vector.scalar_tensor_tensor(out=qf, in0=qf, scalar=float(DK) ** -0.5, in1=gx0,
                                           op0=ALU.mult, op1=ALU.mult)
            dve.wait_ge(s_gs, GP + 3)
            nc.vector.tensor_tensor(gx2, kf, gx2, ALU.mult).then_inc(s_gv, 1)
            dve.wait_ge(s_gs, GP + 4)
            dve.drain()
            nc.vector.tensor_tensor(kf, kf, gx1, ALU.mult).then_inc(s_gv, 1)

            for j, (n, kind, i) in enumerate(jobs):
                if kind not in by_vector:
                    continue
                dve.wait_ge(s_job, j + 1)
                src = bank[j % 4]
                if kind == "ch":
                    at_cc = next(m for m, job in enumerate(jobs) if job[1:] == ("cc", i))
                    dve.wait_ge(s_ja, read_by[at_cc][1])
                    nc.vector.tensor_tensor(uconv[:, i, :], src, cgate[:, i, :], ALU.mult).then_inc(s_jv, 1)
                    dve.drain()
                    continue
                y = mixT[:, i, :]
                tap = [pcol[:, 14 + CC * t + i:15 + CC * t + i] for t in range(3)]
                nc.vector.tensor_scalar(y, uconv[:, i, :], tap[2], None, ALU.mult)
                dve.drain()
                for back in (1, 2):
                    nc.vector.scalar_tensor_tensor(out=y[:, back:SEQ], in0=uconv[:, i, 0:SEQ - back],
                                                   scalar=tap[2 - back], in1=y[:, back:SEQ],
                                                   op0=ALU.mult, op1=ALU.add)
                    dve.drain()
                nc.vector.tensor_tensor(y, y, src, ALU.mult).then_inc(s_jv, 1)

            ebt = gx0.rearrange("p (c t) -> p c t", c=GP)
            nc.vector.memset(attn.rearrange("p i b t -> p (i b t)"), 0.0)
            for i in range(GP):
                dve.wait_ge(s_kv, i + 1)
                kv = (pa, pb)[i][:, :].rearrange("p (o n e) -> p n o e", o=2, e=P)
                nc.vector.tensor_copy(state[:, i, 0, :], kv[:, 0, 0, :])
                dve.drain()
                for n in range(1, NCH - 1):
                    last = nc.vector.scalar_tensor_tensor(
                        out=state[:, i, n, :], in0=state[:, i, n - 1, :],
                        scalar=ebt[:, i, CHUNK * n + CHUNK - 1:CHUNK * (n + 1)], in1=kv[:, n // 2, n % 2, :],
                        op0=ALU.mult, op1=ALU.add)
                    dve.drain() if n < NCH - 2 else last.then_inc(s_st, 1)

            def mask(hd):
                dve.wait_ge(s_at, hd + 1)
                if hd >= 2:
                    dve.wait_ge(s_o, hd - 1)
                keep = causal[:, :].bitcast(U32).unsqueeze(1).to_broadcast((P, NB, P))
                nc.vector.copy_predicated(attn[:, hd % 2], keep,
                                          bank[6 + hd % 2].rearrange("p (b t) -> p b t", b=NB)).then_inc(s_am, 1)

            def normalise(hd):
                dve.wait_ge(s_ms, hd + 1)
                nc.vector.tensor_scalar(rms[:, hd % 2, :], bank[hd % 2], 1.0 / P, RMS_EPS,
                                        ALU.mult, ALU.add).then_inc(s_msv, 1)
                dve.wait_ge(s_rt, hd + 1)
                nc.vector.reciprocal(rms[:, hd % 2, :], rms[:, hd % 2, :])
                dve.drain()
                y = mixT[:, CC + hd, :]
                nc.vector.tensor_tensor(y, bank[4 + hd % 2], rms[:, hd % 2, :], ALU.mult)
                dve.drain()
                nc.vector.scalar_tensor_tensor(out=y, in0=y, scalar=pcol[:, 10 + hd:11 + hd], in1=r_[:, hd, :],
                                               op0=ALU.mult, op1=ALU.mult).then_inc(s_mix, 1)

            dve.drain()
            mask(0)
            mask(1)
            mask(2)
            normalise(0)
            mask(3)
            for hd in range(1, GH):
                normalise(hd)

            def layer_norm(n, y, gate, res, dst, y_read=None):
                first = nc.vector.tensor_tensor(ln_t, y, gate, ALU.mult)
                if y_read is not None:
                    first.then_inc(y_read, 1)
                dve.drain()
                nc.vector.scalar_tensor_tensor(out=ln_t, in0=res, scalar=ALPHA, in1=ln_t, op0=ALU.mult, op1=ALU.add)
                dve.drain()
                for i in range(2):
                    nc.vector.bn_stats(stats[:, i, :], ln_t[:, 512 * i:512 * (i + 1)])
                dve.drain()
                nc.vector.bn_aggr(mv, stats)
                dve.drain()
                nc.vector.tensor_scalar(mv[:, 1:2], mv[:, 1:2], LN_EPS, None, ALU.add).then_inc(s_lv, 1)
                dve.wait_ge(s_ls, n)
                nc.vector.reciprocal(rstd, std)
                dve.drain()
                nc.vector.tensor_scalar(ln_t, ln_t, mv[:, 0:1], rstd, ALU.subtract, ALU.mult)
                dve.drain()
                nc.vector.tensor_tensor(ln_t, ln_t, lng, ALU.mult)
                dve.drain()
                return nc.vector.tensor_tensor(dst, ln_t, lnb, ALU.add)

            def front(b):
                dve.wait_ge(s_wop, b + 1)
                layer_norm(b + 1, pc[:, :], gate1, x_sb[:, b, :], x_sb[:, b, :], y_read=s_lnz)
                dve.drain()
                nc.vector.tensor_tensor(ln_o, x_sb[:, b, :], scale2, ALU.mult)
                dve.drain()
                nc.vector.tensor_tensor(h2[:, b, :], ln_o, shift2, ALU.add).then_inc(s_h2, 1)

            def top16(values, best_, where, rest_):
                nc.vector.max(best_[:, 0:8], values)
                dve.drain()
                nc.vector.max_index(where[:, 0:8], best_[:, 0:8], values)
                last = nc.vector.match_replace(out=rest_, in_to_replace=best_[:, 0:8], in_values=values,
                                               imm_value=LOWEST)
                dve.drain()
                nc.vector.max(best_[:, 8:16], rest_)
                dve.drain()
                nc.vector.max_index(where[:, 8:16], best_[:, 8:16], rest_)
                return last

            def select(g, b):
                par = b % 2
                dve.wait_ge(s_sc, g + 1)
                dve.nop(nofuse=True)
                for p in range(2):
                    last = top16(sps[par][:, p, :], best[:, p, :], besti[:, p, :], rest[:, p, :])
                last.then_inc(s_scr, 1)
                dve.drain()
                nc.vector.tensor_tensor(cand, best[:, 0, :].unsqueeze(2).to_broadcast((P, TOPK, TOPK)),
                                        best[:, 1, :].unsqueeze(1).to_broadcast((P, TOPK, TOPK)), ALU.add)
                nc.vector.tensor_copy(bestf, besti)
                dve.drain()
                top16(cand.rearrange("p a b -> p (a b)"), top[:, par, :], pos, cand2.rearrange("p a b -> p (a b)"))
                nc.vector.tensor_scalar(ntop[:, par, :], top[:, par, 0:1], -1.0, None, ALU.mult).then_inc(s_top, 1)
                dve.drain()
                nc.vector.tensor_scalar(part[:, :, 0], pos, 4, None, ALU.logical_shift_right)
                nc.vector.tensor_scalar(part[:, :, 1], pos, TOPK - 1, None, ALU.bitwise_and)
                dve.drain()
                nc.vector.tensor_copy(partf, part)
                dve.drain()
                whole = (P, TOPK, 2, TOPK)
                nc.vector.tensor_tensor(pick, seq16[:, :].unsqueeze(1).unsqueeze(1).to_broadcast(whole),
                                        partf.unsqueeze(3).to_broadcast(whole), ALU.is_equal)
                dve.drain()
                nc.vector.tensor_tensor(pick, pick, bestf.unsqueeze(1).to_broadcast(whole), ALU.mult)
                dve.drain()
                nc.vector.tensor_reduce(keys, pick, mybir.AxisListType.X, ALU.add)
                dve.drain()
                nc.vector.scalar_tensor_tensor(out=idx[:, b, :], in0=keys[:, :, 0], scalar=float(NKEYS),
                                               in1=keys[:, :, 1], op0=ALU.mult, op1=ALU.add).then_inc(s_idx, 1)
                dve.drain()

            def add_y(g, b, into_new):
                dve.wait_ge(s_vu, 16 * g + 16)
                y = yps[b % 2][:, :]
                if into_new:
                    nc.vector.tensor_copy(yacc[:, b, :], y).then_inc(s_yr, 1)
                else:
                    nc.vector.tensor_tensor(yacc[:, b, :], yacc[:, b, :], y, ALU.add).then_inc(s_yr, 1)

            def slot(h, b, g, more=True, first=False):
                if more:
                    select(g + 1, (b + 1) % NB)
                if first:
                    front(2)
                    front(3)
                for s in range(TOPK):
                    dve.wait_ge(s_u[s % RING], 16 * (2 * g + s // RING + 1))
                    row = u_ring[:, s % RING, :]
                    nc.vector.tensor_tensor_reduce(out=row, in0=row, in1=h2[:, b, :], scale=1.0, scalar=0.0,
                                                   op0=ALU.mult, op1=ALU.add,
                                                   accum_out=dots[:, b % 2, s:s + 1]).then_inc(s_dot, 1)
                dve.wait_ge(s_exp, g + 1)
                nc.vector.reciprocal(rsum, esum[:, b % 2, :])
                dve.drain()
                dve.wait_ge(s_gel, g + 1)
                nc.vector.scalar_tensor_tensor(out=coef[:, b % 2, :], in0=act_[:, b % 2, :], scalar=rsum,
                                               in1=expo[:, b % 2, :], op0=ALU.mult, op1=ALU.mult).then_inc(s_coef, 1)

            def finish(b):
                dve.drain()
                layer_norm(NB + b + 1, yacc[:, b, :], gate2, x_sb[:, b, :], x_sb[:, b, :]).then_inc(s_fin, 1)

            dve.wait_ge(s_lnr, 32)
            dve.wait_ge(s_rbe, 8)
            front(0)
            dve.drain()
            select(0, 0)
            front(1)
            for b in range(NB):
                slot(0, b, b, first=b == 0)
                if b > 0:
                    add_y(b - 1, b - 1, True)
            nc.vector.memset(yacc[:, NB - 1, :], 0.0)
            dve.drain()
            with dve.Fori(1, HEADS - 1) as h:
                for b in range(NB):
                    g = h * NB + b
                    slot(h, b, g)
                    add_y(g - 1, (b - 1) % NB, False)
            dve.wait_ge(s_ln2r, 32)
            for b in range(NB):
                g = NG - NB + b
                slot(HEADS - 1, b, g, more=b < NB - 1)
                add_y(g - 1, (b - 1) % NB, False)
                if b > 0:
                    finish(b - 1)
            add_y(NG - 1, NB - 1, False)
            finish(NB - 1)

        @block.tensor
        def _(pe):
            pe.wait_ge(s_const, 1)
            pe.wait_ge(s_par, 64)
            nc.tensor.transpose(bank[6][:, 0:26], prow[0:26, :], ident[0:26, 0:26]).then_inc(s_colps, 1)
            pe.wait_ge(s_x, 16)
            for k in range(KC):
                if k >= 2:
                    pe.wait_ge(s_xte, k - 1)
                for b in range(NB):
                    mm = nc.tensor.transpose(bank[4 + k % 2][:, b * P:(b + 1) * P], x_sb[:, b, k * P:(k + 1) * P],
                                             ident[:, :])
                mm.then_inc(s_xt, 1)
            pe.wait_ge(s_mu, KC)
            for j in range(2 * KC):
                mm = nc.tensor.matmul(bank[7][:, j:j + 1], mod_cols[:, j * P:(j + 1) * P], ones[:, 0:1],
                                      start=True, stop=True)
            mm.then_inc(s_mc, 1)

            def mod_rows():
                pe.wait_ge(s_mu, MT)
                for j in range(8):
                    if j >= 2:
                        pe.wait_ge(s_rbe, j - 1)
                    nc.tensor.matmul(bank[6 + j % 2], ones[:, :], rows[:, 2 * D + 512 * j:2 * D + 512 * (j + 1)],
                                     start=True, stop=True).then_inc(s_rb, 1)

            def gates():
                pe.wait_ge(s_wq, 16)
                for i in range(GP):
                    nc.tensor.matmul(bank[4 + i], gate_up[:, i * P:(i + 1) * P], glr, start=True,
                                     stop=True).then_inc(s_z, 1)

            for j, (n, kind, i) in enumerate(jobs):
                if j == first_job[n]:
                    pe.wait_ge(s_w[n % 4], 16 * (n // 4 + 1))
                if j >= 4:
                    e, count = read_by[j - 4]
                    pe.wait_ge(s_ja if e == "a" else s_jv, count)
                w = w_ring[:, n % 4]
                if kind == "v":
                    for bb in range(2):
                        b = 2 * i[1] + bb
                        for k in range(KC):
                            mm = nc.tensor.matmul(bank[j % 4][:, WT * bb:WT * (bb + 1)], hT[:, k, b * P:(b + 1) * P],
                                                  w[:, k, :], start=k == 0, stop=k == KC - 1)
                else:
                    m = RANK if kind == "glr" else P
                    lo = 0 if kind == "glr" else P * (j - first_job[n])
                    for k in range(KC):
                        if j == 0:
                            pe.wait_ge(s_h, k + 1)
                        mm = nc.tensor.matmul(bank[j % 4][0:m, :], w[:, k, lo:lo + m], hT[:, k, :],
                                              start=k == 0, stop=k == KC - 1)
                mm.then_inc(s_job, 1)
                if kind == "r" and i == 3:
                    mod_rows()
                    gates()

            pe.wait_ge(s_gv, 3)
            kl = gx2.rearrange("p (c t) -> p c t", c=GP)
            for i in range(GP):
                for b in range(NB):
                    mm = nc.tensor.transpose(bank[4 + i][:, b * P:(b + 1) * P], kl[:, i, b * P:(b + 1) * P],
                                             ident[:, :])
                mm.then_inc(s_klp, 1)
            pe.wait_ge(s_jv, counts["v"])
            for i in range(GP):
                pe.wait_ge(s_klt, i + 1)
                for n in range(NCH - 1):
                    lo = CHUNK * (n % 2)
                    for hh in range(2):
                        hd = 2 * i + hh
                        col = 512 * (n % 2) + P * (n // 2)
                        mm = nc.tensor.matmul((pa, pb)[i][DK * hh:DK * (hh + 1), col:col + P],
                                              klT[lo:lo + CHUNK, i, n // 2, DK * hh:DK * (hh + 1)],
                                              v_[lo:lo + CHUNK, n // 2, hd * P:(hd + 1) * P], start=True, stop=True)
                mm.then_inc(s_kv, 1)

            def scores_of(hd):
                i, lo = hd // 2, DK * (hd % 2)
                if hd >= 2:
                    pe.wait_ge(s_am, hd - 1)
                for b in range(NB):
                    mm = nc.tensor.matmul(bank[6 + hd % 2][:, b * P:(b + 1) * P],
                                          k_[lo:lo + DK, i, b * P:(b + 1) * P],
                                          q_[lo:lo + DK, i, b * P:(b + 1) * P], start=True, stop=True)
                mm.then_inc(s_at, 1)

            def outputs_of(hd):
                i, lo = hd // 2, DK * (hd % 2)
                pe.wait_ge(s_am, hd + 1)
                pe.wait_ge(s_st, i + 1)
                if hd >= 2:
                    pe.wait_ge(s_mix, hd - 1)
                o = bank[4 + hd % 2]
                for b in range(NB):
                    mm = nc.tensor.matmul(o[:, b * P:(b + 1) * P], v_[:, b, hd * P:(hd + 1) * P],
                                          attn[:, hd % 2, b, :], start=True, stop=False, skip_group_check=True)
                    for n in (2 * b, 2 * b + 1):
                        if n == 0:
                            continue
                        mm = nc.tensor.matmul(o[:, n * CHUNK:(n + 1) * CHUNK], state[lo:lo + DK, i, n - 1, :],
                                              q_[lo:lo + DK, i, n * CHUNK:(n + 1) * CHUNK],
                                              start=False, stop=n % 2 == 1, skip_group_check=True)
                mm.then_inc(s_o, 1)

            def mean_square(hd):
                pe.wait_ge(s_sq, hd + 1)
                if hd >= 2:
                    pe.wait_ge(s_msv, hd - 1)
                nc.tensor.matmul(bank[hd % 2], ones[:, :], sq[:, hd % 2, :], start=True, stop=True).then_inc(s_ms, 1)

            pe.wait_ge(s_gv, 4)
            pe.wait_ge(s_rbe, 8)
            scores_of(0)
            scores_of(1)
            outputs_of(0)
            scores_of(2)
            outputs_of(1)
            mean_square(0)
            scores_of(3)
            mean_square(1)
            outputs_of(2)
            mean_square(2)
            outputs_of(3)
            mean_square(3)

            def scores(g, b):
                if not (isinstance(g, int) and g < 2):
                    pe.wait_ge(s_scr, g - 1)
                for p in range(2):
                    mm = nc.tensor.matmul(sps[b % 2][:, p, :], qT[:, p, b * P:(b + 1) * P], skT[:, p, :],
                                          start=True, stop=True)
                mm.then_inc(s_sc, 1)

            def subkeys(h):
                pe.wait_ge(s_wq, 16 * (2 * h + 3))
                for p in range(2):
                    mm = nc.tensor.transpose(pc[:, NKEYS * p:NKEYS * (p + 1)], sk_sb[:, p, :], ident[:, :])
                mm.then_inc(s_skp, 1)

            def front(b):
                if b == 0:
                    pe.wait_ge(s_wo, 16)
                    pe.wait_ge(s_mix, GH)
                else:
                    pe.wait_ge(s_qe, b)
                for half in range(2):
                    for k in range(KC):
                        mm = nc.tensor.matmul(pc[:, 512 * half:512 * (half + 1)], mixT[:, k, b * P:(b + 1) * P],
                                              wout[:, k, 512 * half:512 * (half + 1)], start=k == 0, stop=k == KC - 1)
                mm.then_inc(s_wop, 1)
                pe.wait_ge(s_lnz, b + 1)
                if b == 0:
                    subkeys(0)
                    pe.wait_ge(s_ske, 1)
                pe.wait_ge(s_h2, b + 1)
                for half in range(2):
                    for k in range(4):
                        mm = nc.tensor.transpose(bank[4 + half][:, k * P:(k + 1) * P],
                                                 h2[:, b, (4 * half + k) * P:(4 * half + k + 1) * P], ident[:, :])
                    mm.then_inc(s_tp, 1)
                pe.wait_ge(s_tpe, 2 * b + 2)
                for p in range(2):
                    for k in range(KC):
                        mm = nc.tensor.matmul(pc[:, 512 * p:512 * p + P], wq_sb[:, k, p * P:(p + 1) * P],
                                              hT[:, k, b * P:(b + 1) * P], start=k == 0, stop=k == KC - 1)
                mm.then_inc(s_qp, 1)
                pe.wait_ge(s_qe, b + 1)
                scores(b, b)

            def next_head(h):
                subkeys(h)
                pe.wait_ge(s_ske, h + 1)
                for p in range(2):
                    for k in range(KC):
                        mm = nc.tensor.matmul(pc[:, 512 * p:512 * (p + 1)], wq_sb[:, k, p * P:(p + 1) * P],
                                              hT[:, k, :], start=k == 0, stop=k == KC - 1)
                mm.then_inc(s_qp, 1)

            def weigh(g, b):
                if not (isinstance(g, int) and g < 2):
                    pe.wait_ge(s_yr, g - 1)
                for s in range(TOPK):
                    pe.wait_ge(s_diag, 16 * g + s + 1)
                    pe.wait_ge(s_v[s % RING], 16 * (2 * g + s // RING + 1))
                    for half in range(2):
                        mm = nc.tensor.matmul(yps[b % 2][:, 512 * half:512 * (half + 1)], diag[:, s, :],
                                              v_ring[:, s % RING, 512 * half:512 * (half + 1)],
                                              start=s == 0, stop=s == TOPK - 1)
                    mm.then_inc(s_vu, 1)

            front(0)
            front(1)
            front(2)
            front(3)
            for b in range(1, NB):
                if b == 2:
                    pe.wait_ge(s_qe, NB + 1)
                if b >= 2:
                    scores(b + 2, (b + 2) % NB)
                weigh(b - 1, b - 1)
                if b == 1:
                    next_head(1)
            with pe.Fori(1, HEADS - 1) as h:
                for b in range(NB):
                    g = h * NB + b
                    if b == 2:
                        pe.wait_ge(s_qe, NB + h + 1)
                    scores(g + 2, (b + 2) % NB)
                    weigh(g - 1, (b - 1) % NB)
                    if b == 1:
                        next_head(h + 1)
            for b in range(NB):
                g = NG - NB + b
                if b < 2:
                    scores(g + 2, b + 2)
                weigh(g - 1, (b - 1) % NB)
            weigh(NG - 1, NB - 1)


_INS = ["x", "c", "w_mod", "b_mod", "w_in", "conv_w", "gla_gate_up", "gla_gate_bias", "gla_norm_g", "w_out",
        "ln1_g", "ln1_b", "peer_wq", "peer_subkeys", "peer_u", "peer_v", "ln2_g", "ln2_b"]


def kernel(**inputs):
    import numpy as np
    import concourse.bacc as bacc
    from concourse.bass_utils import run_bass_kernel_spmd

    nc = bacc.Bacc("TRN2", target_bir_lowering=False, num_devices=1)
    arrays, args = {}, []
    for name in _INS:
        a = np.ascontiguousarray(inputs[name])
        arrays[f"in_{name}"] = a
        args.append(nc.dram_tensor(f"in_{name}", a.shape, mybir.dt.from_np(a.dtype), kind="ExternalInput").ap())
    args.append(nc.dram_tensor("out_0", inputs["x"].shape, F32, kind="ExternalOutput").ap())
    build(nc, *args)
    r = run_bass_kernel_spmd(nc, [arrays], core_ids=[0])
    return r.results[0]["out_0"]
```

```python
from contextlib import ExitStack

import concourse.bass as bass
from concourse import mybir

F32 = mybir.dt.float32
U32 = mybir.dt.uint32
ALU = mybir.AluOpType
ACT = mybir.ActivationFunctionType

P = 128
LN_EPS = 1e-5
RMS_EPS = 1e-6
GLA_TAU = 16.0
CHUNK = 64
TOPK = 16
RING = 8
STEP = 2
LOWEST = -3.0e38


def build(nc, x, c, w_mod, b_mod, w_in, conv_w, gla_gate_up, gla_gate_bias, gla_norm_g, w_out,
          ln1_g, ln1_b, peer_wq, peer_subkeys, peer_u, peer_v, ln2_g, ln2_b, out):
    _, SEQ, D = x.shape
    KC = D // P
    NB = SEQ // P
    CW = conv_w.shape[1]
    CC = CW // P
    RANK, GK = gla_gate_up.shape
    GV = gla_norm_g.shape[0]
    GH = GV // P
    GP = GK // P
    DK = GK // GH
    NCH = SEQ // CHUNK
    HEADS, _, NKEYS, HALF = peer_subkeys.shape
    QD = 2 * HALF
    NG = HEADS * NB
    ALPHA = 2.0 ** 0.25
    assert NB == 4 and HALF == P and NKEYS == P

    ctx = ExitStack()
    with ctx:
        def sb(name, shape, dt=F32):
            return ctx.enter_context(nc.sbuf_tensor(name, shape, dt))

        def psum(name):
            return ctx.enter_context(nc.psum_tensor(name, [P, 1024], F32))

        def sem(name):
            return ctx.enter_context(nc.semaphore(name))

        u_ring = sb("u_ring", [P, RING, D])
        v_ring = sb("v_ring", [P, RING, D])
        x_sb = sb("x_sb", [P, NB, D])
        hT = sb("hT", [P, KC, SEQ])
        h2 = sb("h2", [P, NB, D])
        mixT = sb("mixT", [P, KC, SEQ])
        rows = sb("rows", [P, 6 * D])
        mid = sb("mid", [P, 6656])
        gx = sb("gx", [P, 3 * 1024])
        wq_sb = sb("wq_sb", [P, KC, QD])
        misc = sb("misc", [P, 2 * SEQ])
        ident = sb("ident", [P, P])
        ones = sb("ones", [P, P])
        causal = sb("causal", [P, P])
        prow = sb("prow", [32, P])
        pcol = sb("pcol", [P, 32])
        siluc = sb("siluc", [P, KC])
        modc = sb("modc", [P, 2 * KC])
        gate_up = sb("gate_up", [RANK, GK])

        w_ring = u_ring[:, :, :].rearrange("p a b -> p (a b)").rearrange("p (s k c) -> p s k c", s=4, k=KC)
        m_ring = v_ring[:, :, :].rearrange("p a b -> p (a b)").rearrange("p (s c) -> p s c", s=4)
        wout = v_ring
        h2f = h2[:, :, :].rearrange("p a b -> p (a b)")
        cgate = h2f[:, 0:CC * SEQ].rearrange("p (c t) -> p c t", c=CC)
        uconv = h2f[:, CC * SEQ:2 * CC * SEQ].rearrange("p (c t) -> p c t", c=CC)
        q_ = mid[:, 0:1024].rearrange("p (c t) -> p c t", c=GP)
        k_ = mid[:, 1024:2048].rearrange("p (c t) -> p c t", c=GP)
        v_ = mid[:, 2048:4096].rearrange("p (b e) -> p b e", b=NB)
        r_ = mid[:, 4096:6144].rearrange("p (h t) -> p h t", h=GH)
        glr = mid[0:RANK, 6144:6656]
        gx0, gx1, gx2 = (gx[:, 1024 * i:1024 * (i + 1)] for i in range(3))
        restart = misc[:, SEQ:2 * SEQ]
        attn = misc[:, :].rearrange("p (i b t) -> p i b t", i=2, b=NB)
        wqf = wq_sb[:, :, :].rearrange("p k c -> p (k c)")
        klT = wqf[:, 0:1024].rearrange("p (c b d) -> p c b d", c=GP, b=NB)
        state = [wqf[:, o:o + (NCH - 1) * P].rearrange("p (n e) -> p n e", e=P) for o in (1024, 0)]
        sq = gx1.rearrange("p (i t) -> p i t", i=2)
        rms = gx2.rearrange("p (i t) -> p i t", i=2)

        diag = mid[:, 0:2048].rearrange("p (s t) -> p s t", s=TOPK)
        ln_ts = [mid[:, 2048:3072], mid[:, 5120:6144]]
        fold_tmp = mixT[:, KC - 2:KC, :].rearrange("p k t -> p (k t)")
        qT = mid[:, 4096:5120].rearrange("p (a t) -> p a t", a=2)
        sk_sb = misc[:, 0:2 * HALF].rearrange("p (a n) -> p a n", a=2)
        skT = misc[:, 2 * HALF:4 * HALF].rearrange("p (a n) -> p a n", a=2)
        yacc = mixT[:, :, :].rearrange("p a b -> p (a b)").rearrange("p (b d) -> p b d", b=NB)
        at = [0]

        def small(shape, dt=F32):
            n = 1
            for s in shape:
                n *= s
            v = gx[:, at[0]:at[0] + n]
            at[0] += n
            if dt is not F32:
                v = v.bitcast(dt)
            if len(shape) == 2:
                v = v.rearrange("p (a b) -> p a b", a=shape[0])
            if len(shape) == 3:
                v = v.rearrange("p (a b c) -> p a b c", a=shape[0], b=shape[1])
            return v

        rest = small([2, NKEYS])
        best = small([2, TOPK])
        besti = small([2, TOPK], U32)
        bestf = small([2, TOPK])
        cand = small([TOPK, TOPK])
        cand2 = small([TOPK, TOPK])
        pos = small([TOPK], U32)
        part = small([TOPK, 2], U32)
        partf = small([TOPK, 2])
        pick = small([TOPK, 2, TOPK])
        keys = small([TOPK, 2])
        top = small([2, TOPK])
        ntop = small([2, 1])
        expo = small([2, TOPK])
        esum = small([2, 1])
        rsum = small([1])
        dots = small([2, TOPK])
        act_ = small([2, TOPK])
        coef = small([2, TOPK])
        stats = small([2, 6])
        mv = small([2])
        std = small([1])
        rstd = small([1])
        seq16 = sb("seq16", [P, TOPK])
        idx = sb("idx", [P, NB, TOPK], U32)

        mod_cols = rows[:, 0:2 * D]
        lng, lnb = rows[:, 0:D], rows[:, D:2 * D]
        gate1, shift2, scale2, gate2 = (rows[:, D * i:D * (i + 1)] for i in (2, 3, 4, 5))

        pa, pb, pc, pd = psum("pa"), psum("pb"), psum("pc"), psum("pd")
        bank = [t[:, 512 * i:512 * (i + 1)] for t in (pa, pb, pc, pd) for i in range(2)]
        yps = [pa, pb]
        sps = [pd[:, 512 * i:512 * i + 256].rearrange("p (a n) -> p a n", a=2) for i in range(2)]

        s_par = sem("params_landed")
        s_bmod = sem("b_mod_landed")
        s_x = sem("x_landed")
        s_m = [sem(f"w_mod_landed{i}") for i in range(4)]
        s_w = [sem(f"w_in_landed{i}") for i in range(4)]
        s_lnr = sem("ln_rows_landed")
        s_ln2r = sem("ln2_rows_landed")
        s_wo = sem("w_out_landed")
        s_wq = sem("wq_landed")
        s_u = [sem(f"u_landed{i}") for i in range(RING)]
        s_v = [sem(f"v_landed{i}") for i in range(RING)]
        s_out = sem("out_stored")
        s_const = sem("constants_made")
        s_zero = sem("rows_zeroed")
        s_colps = sem("param_columns_in_psum")
        s_col = sem("param_columns_ready")
        s_xt = sem("x_transposed")
        s_xte = sem("x_transposes_copied")
        s_mu = sem("w_mod_tile_used")
        s_mc = sem("mod_columns_in_psum")
        s_mce = sem("mod_columns_ready")
        s_h = sem("hT_ready")
        s_job = sem("projection_in_psum")
        s_ja = sem("projection_copied_by_scalar")
        s_jv = sem("projection_read_by_vector")
        s_rb = sem("mod_rows_in_psum")
        s_rbe = sem("mod_rows_ready")
        s_z = sem("gate_in_psum")
        s_gs = sem("gate_step_of_scalar")
        s_gv = sem("gate_step_of_vector")
        s_klp = sem("klT_in_psum")
        s_klt = sem("klT_ready")
        s_kv = sem("kv_in_psum")
        s_st = sem("state_ready")
        s_at = sem("scores_of_attention_in_psum")
        s_am = sem("attention_masked")
        s_o = sem("o_in_psum")
        s_sq = sem("o_squared")
        s_ms = sem("mean_square_in_psum")
        s_msv = sem("mean_square_read")
        s_rt = sem("rms_root_ready")
        s_mix = sem("mix_ready")
        s_wg = sem("w_out_rows_gated")
        s_fold = sem("h2_rows_folded")
        s_x1g = sem("x1_product_ready")
        s_x1 = sem("x1_ready")
        s_wop = sem("w_out_product_in_psum")
        s_lv = sem("ln_variance_ready")
        s_ls = sem("ln_std_ready")
        s_lnz = sem("w_out_product_read")
        s_h2 = sem("h2_ready")
        s_tp = sem("h2_transposed")
        s_tpe = sem("h2T_ready")
        s_skp = sem("subkeys_transposed")
        s_ske = sem("subkeysT_ready")
        s_qp = sem("query_in_psum")
        s_qe = sem("query_ready")
        s_sc = sem("scores_in_psum")
        s_scr = sem("scores_read")
        s_top = sem("top_ready")
        s_exp = sem("exp_ready")
        s_idx = sem("idx_ready")
        s_dot = sem("dot_done")
        s_gel = sem("gelu_ready")
        s_coef = sem("coef_ready")
        s_diag = sem("diag_ready")
        s_vu = sem("v_rows_used")
        s_yr = sem("y_read")
        s_fin = sem("result_ready")

        WT = 256
        tiles = [12, 6, 7, 8, 9, 10, 11, 2, 4, 0, 3, 5, 1]
        q_tile, k_tile, v_tile, r_tile, g_tile = 6, 7, 8, 10, 12
        jobs = []
        for n, t in enumerate(tiles):
            if t == g_tile:
                jobs.append((n, "glr", 0))
            elif t == q_tile or t == k_tile:
                jobs += [(n, "q" if t == q_tile else "k", i) for i in range(2)]
            elif v_tile <= t < v_tile + 2:
                jobs += [(n, "v", (t - v_tile, i)) for i in range(2)]
            elif r_tile <= t < r_tile + 2:
                jobs += [(n, "r", 2 * (t - r_tile) + i) for i in range(2)]
            else:
                kind = ("cb", "cc", "ch")[t // 2]
                jobs += [(n, kind, 2 * (t % 2) + i) for i in range(2)]
        by_vector = ("cb", "ch")
        read_by, counts = [], {"a": 0, "v": 0}
        for _, kind, _ in jobs:
            e = "v" if kind in by_vector else "a"
            counts[e] += 1
            read_by.append((e, counts[e]))
        n_attn = sum(kind not in ("cb", "cc", "ch") for _, kind, _ in jobs)
        job_bank = [j % 4 if j < n_attn else (j - n_attn) % 2 for j in range(len(jobs))]
        before = [max((m for m in range(j) if job_bank[m] == job_bank[j]), default=None) for j in range(len(jobs))]
        first_job = [min(j for j, job in enumerate(jobs) if job[0] == n) for n in range(len(tiles))]
        last_job = [max(j for j, job in enumerate(jobs) if job[0] == n) for n in range(len(tiles))]
        MT = 3 * KC

        def mod_tile(i):
            return (i, 0) if i < KC else ((i - KC) // 2, 2 * D * (1 + (i - KC) % 2))

        block = ctx.enter_context(nc.Block())

        @block.sync
        def _(sp):
            sp.dma_start(prow[0:8, :], c.rearrange("a (k p) -> (a k) p", p=P)).then_inc(s_par, 16)
            sp.dma_start(prow[8:10, :], gla_gate_bias.rearrange("(k p) -> k p", p=P)).then_inc(s_par, 16)
            sp.dma_start(prow[10:14, :], gla_norm_g.rearrange("(k p) -> k p", p=P)).then_inc(s_par, 16)
            sp.dma_start(prow[14:26, :], conv_w.rearrange("j (k p) -> (j k) p", p=P)).then_inc(s_par, 16)

            def load_mod(i):
                k, col = mod_tile(i)
                if i >= 4:
                    sp.wait_ge(s_mu, i - 3)
                sp.dma_start(m_ring[:, i % 4, :], w_mod[k * P:(k + 1) * P, col:col + 2 * D]).then_inc(s_m[i % 4], 16)

            def load_win(n):
                if n >= 4:
                    sp.wait_ge(s_job, last_job[n - 4] + 1)
                col = WT * tiles[n]
                width = min(WT, w_in.shape[1] - col)
                sp.dma_start(w_ring[:, n % 4, :, 0:width],
                             w_in[:, col:col + width].rearrange("(k p) c -> p k c", p=P)).then_inc(s_w[n % 4], 16)

            for i in range(4):
                load_mod(i)
            sp.wait_ge(s_zero, 1)
            sp.dma_start(rows[0:1, :], b_mod.rearrange("(a n) -> a n", a=1)).then_inc(s_bmod, 16)
            sp.dma_start(x_sb[:, :, :], x[0].rearrange("(b p) d -> p b d", p=P)).then_inc(s_x, 16)
            for i in range(4, KC):
                load_mod(i)
            sp.dma_start(gate_up[:, :], gla_gate_up).then_inc(s_wq, 16)
            for n in range(4):
                load_win(n)
            i = KC
            for n in range(4, len(tiles)):
                for _ in range(6 if n == 4 else 4):
                    if i < MT:
                        load_mod(i)
                        i += 1
                load_win(n)
                if n == 7:
                    sp.wait_ge(s_mce, 1)
                    sp.dma_start(lng, ln1_g.partition_broadcast(P)).then_inc(s_lnr, 16)
                    sp.dma_start(lnb, ln1_b.partition_broadcast(P)).then_inc(s_lnr, 16)
                if n == 9:
                    sp.wait_ge(s_mu, MT)
                    sp.dma_start(wout[:, :, :], w_out.rearrange("(k p) n -> p k n", p=P)).then_inc(s_wo, 16)
            sp.wait_ge(s_o, GH)
            sp.dma_start(wq_sb[:, :, :], peer_wq[:, 0:QD].rearrange("(k p) c -> p k c", p=P)).then_inc(s_wq, 16)
            sp.dma_start(sk_sb, peer_subkeys[0].rearrange("a n d -> n a d")).then_inc(s_wq, 16)
            sp.wait_ge(s_qe, NB)
            with sp.Fori(1, HEADS) as h:
                sp.wait_ge(s_ske, h)
                sp.dma_start(wq_sb[:, :, :], peer_wq[:, bass.ds(h * QD, QD)].rearrange("(k p) c -> p k c", p=P)).then_inc(s_wq, 16)
                sp.dma_start(sk_sb, peer_subkeys[bass.ds(h, 1)].rearrange("o a n d -> n (o a) d")).then_inc(s_wq, 16)
            sp.wait_ge(s_x1, NB)
            sp.dma_start(lng, ln2_g.partition_broadcast(P)).then_inc(s_ln2r, 16)
            sp.dma_start(lnb, ln2_b.partition_broadcast(P)).then_inc(s_ln2r, 16)
            for b in range(NB):
                sp.wait_ge(s_fin, b + 1)
                sp.dma_start(out[0, b * P:(b + 1) * P, :], x_sb[:, b, :]).then_inc(s_out, 16)
            sp.wait_ge(s_out, 16 * NB)

        @block.gpsimd
        def _(pool):
            nc.gpsimd.memset(rows[:, :], 0.0).then_inc(s_zero, 1)
            nc.gpsimd.memset(ident[:, :], 0.0)
            nc.gpsimd.memset(ones[:, :], 1.0)
            nc.gpsimd.memset(causal[:, :], 1.0)
            nc.gpsimd.memset(restart, 1.0)
            nc.gpsimd.iota(seq16[:, :], [[1, TOPK]], base=0, channel_multiplier=0,
                           allow_small_or_imprecise_dtypes=True)
            pool.drain()
            nc.gpsimd.affine_select(out=ident[:, :], in_=ident[:, :], compare_op=ALU.not_equal, fill=1.0,
                                    base=0, pattern=[[-1, P]], channel_multiplier=1)
            nc.gpsimd.affine_select(out=causal[:, :], in_=causal[:, :], compare_op=ALU.is_ge, fill=0.0,
                                    base=0, pattern=[[1, P]], channel_multiplier=-1)
            nc.gpsimd.memset(restart.rearrange("p (n t) -> p n t", t=CHUNK)[:, :, 0:1], 0.0)
            pool.drain()
            nc.gpsimd.memset(causal[0:CHUNK, CHUNK:P], 0.0).then_inc(s_const, 1)

            def gather(ring, table, idx_col, landed):
                pool.indirect_dma_start(ring, None, table[:, :],
                                        bass.IndirectOffsetOnAxis(ap=idx_col, axis=0)).then_inc(landed, 16)

            def gather_u(b, s):
                gather(u_ring[:, s % RING, :], peer_u, idx[:, b, s:s + 1], s_u[s % RING])

            def gather_v(b, s):
                gather(v_ring[:, s % RING, :], peer_v, idx[:, b, s:s + 1], s_v[s % RING])

            def x1(b, half):
                if half == 0:
                    pool.wait_ge(s_h2, b + 1)
                    nc.gpsimd.tensor_tensor(x_sb[:, b, :], x_sb[:, b, :], lng, ALU.mult).then_inc(s_x1g, 1)
                else:
                    pool.wait_ge(s_x1g, b + 1)
                    nc.gpsimd.tensor_tensor(x_sb[:, b, :], x_sb[:, b, :], lnb, ALU.add).then_inc(s_x1, 1)

            def slot(h, b, g, u=True, v=True, x1_blocks=()):
                if u:
                    pool.wait_ge(s_idx, g + 1)
                    pool.nop(nofuse=True)
                for s in range(TOPK):
                    if u and s % STEP == 0 and not (g is 0 and s < RING):
                        pool.wait_ge(s_dot, 16 * g + s + STEP - RING)
                        pool.nop(nofuse=True)
                    if u:
                        gather_u(b, s)
                    if v and s % STEP == 0:
                        pool.wait_ge(s_vu, 16 * (g - 1) + s + STEP - RING)
                        pool.nop(nofuse=True)
                    if v:
                        gather_v((b - 1) % NB, s)
                    if x1_blocks and s % 4 == 3:
                        x1(x1_blocks[s // 8], s // 4 % 2)

            def times(dst, a, b):
                return nc.gpsimd.tensor_tensor(dst, a, b, ALU.mult)

            def plus(dst, a, b):
                return nc.gpsimd.tensor_tensor(dst, a, b, ALU.add)

            pool.wait_ge(s_rbe, 8)
            pool.wait_ge(s_lnr, 32)
            times(fold_tmp, lnb, scale2)
            pool.drain()
            plus(shift2, shift2, fold_tmp)
            times(scale2, scale2, lng).then_inc(s_fold, 1)
            pool.wait_ge(s_wo, 16)
            for k in range(KC):
                times(wout[:, k, :], wout[:, k, :], gate1).then_inc(s_wg, 1)

            slot(0, 0, 0, v=False)
            pool.wait_ge(s_wop, NB)
            pool.nop(nofuse=True)
            for s in range(RING):
                gather_v(0, s)
            pool.wait_ge(s_idx, 2)
            pool.nop(nofuse=True)
            for s in range(TOPK):
                if s % STEP == 0:
                    pool.wait_ge(s_dot, 16 + s + STEP - RING)
                    pool.nop(nofuse=True)
                gather_u(1, s)
                if s < RING:
                    if s % STEP == 0:
                        pool.wait_ge(s_vu, s + STEP)
                        pool.nop(nofuse=True)
                    gather_v(0, s + RING)
            for b in range(2, NB):
                slot(0, b, b, x1_blocks=(2 * b - 4, 2 * b - 3))
            with pool.Fori(1, HEADS) as h:
                for b in range(NB):
                    slot(h, b, h * NB + b)
            slot(HEADS, 0, NG, u=False)

        @block.scalar
        def _(act):
            def copy(dst, src):
                return nc.scalar.activation(dst, src, ACT.Copy)

            act.wait_ge(s_colps, 1)
            copy(pcol[:, 0:26], bank[6][:, 0:26])
            act.drain()
            nc.scalar.activation(siluc[:, :], pcol[:, 0:KC], ACT.Silu).then_inc(s_col, 1)
            for k in range(KC):
                act.wait_ge(s_xt, k + 1)
                copy(hT[:, k, :], bank[4 + k % 2]).then_inc(s_xte, 1)
            act.wait_ge(s_mc, 1)
            copy(modc[:, 0:KC], bank[7][:, 0:KC])
            nc.scalar.activation(modc[:, KC:2 * KC], bank[7][:, KC:2 * KC], ACT.Identity, bias=1.0).then_inc(s_mce, 1)
            act.drain()
            for k in range(KC):
                nc.scalar.activation(hT[:, k, :], hT[:, k, :], ACT.Identity, bias=modc[:, k:k + 1],
                                     scale=modc[:, KC + k:KC + k + 1]).then_inc(s_h, 1)

            def mod_rows():
                for j in range(8):
                    act.wait_ge(s_rb, j + 1)
                    plus = 0.0 if j // 2 == 1 else 1.0
                    nc.scalar.activation(rows[:, 2 * D + 512 * j:2 * D + 512 * (j + 1)], bank[6 + j % 2],
                                         ACT.Identity, bias=plus).then_inc(s_rbe, 1)

            def gate_logs():
                zz = gx0.rearrange("p (c t) -> p c t", c=GP)
                for i in range(GP):
                    act.wait_ge(s_z, i + 1)
                    nc.scalar.activation(zz[:, i, :], bank[4 + i], ACT.Identity, bias=pcol[:, 8 + i:9 + i])
                act.drain()
                nc.scalar.activation(gx1, gx0, ACT.Abs)
                act.drain()
                nc.scalar.activation(gx1, gx1, ACT.Exp, scale=-1.0)
                act.drain()
                nc.scalar.activation(gx1, gx1, ACT.Ln, bias=1.0).then_inc(s_gs, 1)

            def gate_exps():
                act.wait_ge(s_gv, 1)
                nc.scalar.activation(gx0, gx1, ACT.Exp, scale=1.0 / GLA_TAU).then_inc(s_gs, 1)
                act.wait_ge(s_gv, 2)
                nc.scalar.activation(gx2, gx2, ACT.Exp, scale=1.0 / GLA_TAU).then_inc(s_gs, 1)
                nc.scalar.activation(gx1, gx1, ACT.Exp, scale=-1.0 / GLA_TAU).then_inc(s_gs, 1)

            def copy_job(j):
                _, kind, i = jobs[j]
                act.wait_ge(s_job, j + 1)
                src = bank[job_bank[j]]
                if kind == "glr":
                    copy(glr, src[0:RANK, :]).then_inc(s_ja, 1)
                elif kind == "q":
                    copy(q_[:, i, :], src).then_inc(s_ja, 1)
                elif kind == "k":
                    copy(k_[:, i, :], src).then_inc(s_ja, 1)
                elif kind == "v":
                    copy(v_[:, 2 * i[1]:2 * i[1] + 2, WT * i[0]:WT * (i[0] + 1)],
                         src.rearrange("p (b e) -> p b e", b=2)).then_inc(s_ja, 1)
                elif kind == "r":
                    nc.scalar.activation(r_[:, i, :], src, ACT.Silu).then_inc(s_ja, 1)
                else:
                    copy(cgate[:, i, :], src).then_inc(s_ja, 1)

            def square(hd):
                act.wait_ge(s_o, hd + 1)
                nc.scalar.activation(sq[:, hd % 2, :], bank[4 + hd % 2], ACT.Square).then_inc(s_sq, 1)

            def root(hd):
                act.wait_ge(s_msv, hd + 1)
                nc.scalar.activation(rms[:, hd % 2, :], rms[:, hd % 2, :], ACT.Sqrt).then_inc(s_rt, 1)

            for j in range(n_attn):
                copy_job(j)
                if j == 2:
                    gate_logs()
                if j == n_attn - 3:
                    gate_exps()
            mod_rows()
            conv = n_attn
            copy_job(conv)
            for i in range(GP):
                act.wait_ge(s_klp, i + 1)
                copy(klT[:, i].rearrange("p b d -> p (b d)"), bank[4 + i]).then_inc(s_klt, 1)
            copy_job(conv + 1)
            square(0)
            square(1)
            root(0)
            root(1)
            square(2)
            copy_job(conv + 6)
            root(2)
            square(3)
            copy_job(conv + 7)
            root(3)
            def ln_root(n):
                act.wait_ge(s_lv, n)
                nc.scalar.activation(std, mv[:, 1:2], ACT.Sqrt).then_inc(s_ls, 1)

            def copy_subkeys(h):
                act.wait_ge(s_skp, h + 1)
                copy(skT[:, :, :].rearrange("p a n -> p (a n)"), pc[:, 0:2 * NKEYS]).then_inc(s_ske, 1)

            def turned(b):
                act.wait_ge(s_tp, b + 1)
                copy(hT[:, :, b * P:(b + 1) * P],
                     pc[:, :].rearrange("p (k t) -> p k t", k=KC)).then_inc(s_tpe, 1)

            def query(b):
                act.wait_ge(s_qp, b + 1)
                copy(qT[:, :, b * P:(b + 1) * P],
                     pc[:, :].rearrange("p (a t) -> p a t", a=2)[:, :, 0:P]).then_inc(s_qe, 1)

            def softmax_top(g, par):
                act.wait_ge(s_top, g + 1)
                nc.scalar.activation(expo[:, par, :], top[:, par, :], ACT.Exp, bias=ntop[:, par, :],
                                     accum_out=esum[:, par, :]).then_inc(s_exp, 1)

            def gelu(b, g):
                act.wait_ge(s_dot, 16 * g + 16)
                nc.scalar.activation(act_[:, b % 2, :], dots[:, b % 2, :], ACT.Gelu).then_inc(s_gel, 1)

            def diagonals(b, g):
                act.wait_ge(s_coef, g + 1)
                for s in range(TOPK):
                    if g is not 0:
                        act.wait_ge(s_vu, 16 * (g - 1) + s + 1)
                    nc.scalar.activation(diag[:, s, :], ident[:, :], ACT.Copy,
                                         scale=coef[:, b % 2, s:s + 1]).then_inc(s_diag, 1)

            def slot(b, g, more=True):
                if more:
                    softmax_top(g + 1, (b + 1) % 2)
                gelu(b, g)
                diagonals(b, g)

            def next_head(h):
                act.wait_ge(s_qp, NB + h)
                copy(qT[:, :, :].rearrange("p a t -> p (a t)"), pc[:, :]).then_inc(s_qe, 1)
                copy_subkeys(h)

            ln_root(1)
            copy_subkeys(0)
            turned(0)
            query(0)
            softmax_top(0, 0)
            ln_root(2)
            turned(1)
            gelu(0, 0)
            query(1)
            diagonals(0, 0)
            softmax_top(1, 1)
            ln_root(3)
            ln_root(4)
            for b in range(2, NB):
                turned(b)
                query(b)
            for b in range(1, NB):
                slot(b, b)
                if b == 1:
                    next_head(1)
            with act.Fori(1, HEADS - 1) as h:
                for b in range(NB):
                    slot(b, h * NB + b)
                    if b == 1:
                        next_head(h + 1)
            for b in range(NB):
                slot(b, NG - NB + b, more=b < NB - 1)
                if b > 0:
                    ln_root(NB + b)
            ln_root(2 * NB)

        @block.vector
        def _(dve):
            dve.wait_ge(s_col, 1)
            dve.wait_ge(s_bmod, 16)
            for i in range(MT):
                k, col = mod_tile(i)
                dve.wait_ge(s_m[i % 4], 16 * (i // 4 + 1))
                acc = rows[:, col:col + 2 * D]
                nc.vector.scalar_tensor_tensor(out=acc, in0=m_ring[:, i % 4, :], scalar=siluc[:, k:k + 1],
                                               in1=acc, op0=ALU.mult, op1=ALU.add).then_inc(s_mu, 1)
                dve.drain()

            dve.wait_ge(s_gs, 1)
            nc.vector.scalar_tensor_tensor(out=gx0, in0=gx0, scalar=0.0, in1=gx1, op0=ALU.min, op1=ALU.subtract)
            dve.drain()
            for i in range(GP):
                last = nc.vector.tensor_tensor_scan(gx1[:, SEQ * i:SEQ * (i + 1)], restart,
                                                    gx0[:, SEQ * i:SEQ * (i + 1)], 0.0, ALU.mult, ALU.add)
            last.then_inc(s_gv, 1)
            dve.drain()
            bch = gx1.rearrange("p (n t) -> p n t", t=CHUNK)
            nc.vector.tensor_tensor(gx2.rearrange("p (n t) -> p n t", t=CHUNK),
                                    bch[:, :, CHUNK - 1:CHUNK].to_broadcast((P, GP * NCH, CHUNK)),
                                    bch, ALU.subtract).then_inc(s_gv, 1)
            nc.vector.memset(attn.rearrange("p i b t -> p (i b t)"), 0.0)
            dve.wait_ge(s_gs, 2)
            qf, kf = mid[:, 0:1024], mid[:, 1024:2048]
            nc.vector.scalar_tensor_tensor(out=qf, in0=qf, scalar=float(DK) ** -0.5, in1=gx0,
                                           op0=ALU.mult, op1=ALU.mult)
            dve.wait_ge(s_gs, 3)
            nc.vector.tensor_tensor(gx2, kf, gx2, ALU.mult).then_inc(s_gv, 1)
            dve.wait_ge(s_gs, 4)
            dve.drain()
            nc.vector.tensor_tensor(kf, kf, gx1, ALU.mult).then_inc(s_gv, 1)

            def conv_job(j):
                _, kind, i = jobs[j]
                dve.wait_ge(s_job, j + 1)
                src = bank[job_bank[j]]
                if kind == "ch":
                    at_cc = next(m for m, job in enumerate(jobs) if job[1:] == ("cc", i))
                    dve.wait_ge(s_ja, read_by[at_cc][1])
                    nc.vector.tensor_tensor(uconv[:, i, :], src, cgate[:, i, :], ALU.mult).then_inc(s_jv, 1)
                    return
                y = mixT[:, i, :]
                tap = [pcol[:, 14 + CC * t + i:15 + CC * t + i] for t in range(3)]
                dve.drain()
                nc.vector.tensor_scalar(y, uconv[:, i, :], tap[2], None, ALU.mult)
                dve.drain()
                for back in (1, 2):
                    nc.vector.scalar_tensor_tensor(out=y[:, back:SEQ], in0=uconv[:, i, 0:SEQ - back],
                                                   scalar=tap[2 - back], in1=y[:, back:SEQ],
                                                   op0=ALU.mult, op1=ALU.add)
                    dve.drain()
                nc.vector.tensor_tensor(y, y, src, ALU.mult).then_inc(s_jv, 1)

            ebt = gx0.rearrange("p (c t) -> p c t", c=GP)

            def states(i):
                dve.wait_ge(s_kv, i + 1)
                kv = pb[:, :].rearrange("p (o n e) -> p n o e", o=2, e=P)
                nc.vector.tensor_copy(state[i][:, 0, :], kv[:, 0, 0, :])
                dve.drain()
                for n in range(1, NCH - 1):
                    last = nc.vector.scalar_tensor_tensor(
                        out=state[i][:, n, :], in0=state[i][:, n - 1, :],
                        scalar=ebt[:, i, CHUNK * n + CHUNK - 1:CHUNK * (n + 1)], in1=kv[:, n // 2, n % 2, :],
                        op0=ALU.mult, op1=ALU.add)
                    dve.drain() if n < NCH - 2 else last.then_inc(s_st, 1)

            def mask(hd):
                dve.wait_ge(s_at, hd + 1)
                if hd >= 2:
                    dve.wait_ge(s_o, hd - 1)
                keep = causal[:, :].bitcast(U32).unsqueeze(1).to_broadcast((P, NB, P))
                nc.vector.copy_predicated(attn[:, hd % 2], keep,
                                          bank[6 + hd % 2].rearrange("p (b t) -> p b t", b=NB)).then_inc(s_am, 1)

            def normalise(hd):
                dve.wait_ge(s_ms, hd + 1)
                nc.vector.tensor_scalar(rms[:, hd % 2, :], bank[2 + hd % 2], 1.0 / P, RMS_EPS,
                                        ALU.mult, ALU.add).then_inc(s_msv, 1)
                dve.wait_ge(s_rt, hd + 1)
                nc.vector.reciprocal(rms[:, hd % 2, :], rms[:, hd % 2, :])
                dve.drain()
                y = mixT[:, CC + hd, :]
                nc.vector.tensor_tensor(y, bank[4 + hd % 2], rms[:, hd % 2, :], ALU.mult)
                dve.drain()
                nc.vector.scalar_tensor_tensor(out=y, in0=y, scalar=pcol[:, 10 + hd:11 + hd], in1=r_[:, hd, :],
                                               op0=ALU.mult, op1=ALU.mult).then_inc(s_mix, 1)

            conv = n_attn
            states(0)
            conv_job(conv + 2)
            states(1)
            mask(0)
            mask(1)
            conv_job(conv + 3)
            mask(2)
            conv_job(conv + 4)
            mask(3)
            normalise(0)
            conv_job(conv + 5)
            normalise(1)
            dve.wait_ge(s_fold, 1)
            normalise(2)
            normalise(3)
            for j in range(conv + 8, conv + 12):
                conv_job(j)

            def standardise(n, ln_t, dst):
                for i in range(2):
                    nc.vector.bn_stats(stats[:, i, :], ln_t[:, 512 * i:512 * (i + 1)])
                dve.drain()
                nc.vector.bn_aggr(mv, stats)
                dve.drain()
                nc.vector.tensor_scalar(mv[:, 1:2], mv[:, 1:2], LN_EPS, None, ALU.add).then_inc(s_lv, 1)
                dve.wait_ge(s_ls, n)
                nc.vector.reciprocal(rstd, std)
                dve.drain()
                nc.vector.tensor_scalar(dst, ln_t, mv[:, 0:1], rstd, ALU.subtract, ALU.mult)
                dve.drain()

            def add_x(b):
                dve.wait_ge(s_wop, b + 1)
                nc.vector.scalar_tensor_tensor(out=ln_ts[b % 2], in0=x_sb[:, b, :], scalar=ALPHA,
                                               in1=yps[(b + 1) % 2][:, :],
                                               op0=ALU.mult, op1=ALU.add).then_inc(s_lnz, 1)
                dve.drain()

            def front(b):
                standardise(b + 1, ln_ts[b % 2], x_sb[:, b, :])
                nc.vector.tensor_tensor(h2[:, b, :], x_sb[:, b, :], scale2, ALU.mult)
                dve.drain()
                nc.vector.tensor_tensor(h2[:, b, :], h2[:, b, :], shift2, ALU.add).then_inc(s_h2, 1)
                dve.drain()

            def top16(values, best_, where, rest_):
                nc.vector.max(best_[:, 0:8], values)
                dve.drain()
                nc.vector.max_index(where[:, 0:8], best_[:, 0:8], values)
                last = nc.vector.match_replace(out=rest_, in_to_replace=best_[:, 0:8], in_values=values,
                                               imm_value=LOWEST)
                dve.drain()
                nc.vector.max(best_[:, 8:16], rest_)
                dve.drain()
                nc.vector.max_index(where[:, 8:16], best_[:, 8:16], rest_)
                return last

            def select(g, b):
                par = b % 2
                dve.wait_ge(s_sc, g + 1)
                dve.nop(nofuse=True)
                for p in range(2):
                    last = top16(sps[par][:, p, :], best[:, p, :], besti[:, p, :], rest[:, p, :])
                last.then_inc(s_scr, 1)
                dve.drain()
                nc.vector.tensor_tensor(cand, best[:, 0, :].unsqueeze(2).to_broadcast((P, TOPK, TOPK)),
                                        best[:, 1, :].unsqueeze(1).to_broadcast((P, TOPK, TOPK)), ALU.add)
                nc.vector.tensor_copy(bestf, besti)
                dve.drain()
                top16(cand.rearrange("p a b -> p (a b)"), top[:, par, :], pos, cand2.rearrange("p a b -> p (a b)"))
                nc.vector.tensor_scalar(ntop[:, par, :], top[:, par, 0:1], -1.0, None, ALU.mult).then_inc(s_top, 1)
                dve.drain()
                nc.vector.tensor_scalar(part[:, :, 0], pos, 4, None, ALU.logical_shift_right)
                nc.vector.tensor_scalar(part[:, :, 1], pos, TOPK - 1, None, ALU.bitwise_and)
                dve.drain()
                nc.vector.tensor_copy(partf, part)
                dve.drain()
                whole = (P, TOPK, 2, TOPK)
                nc.vector.tensor_tensor(pick, seq16[:, :].unsqueeze(1).unsqueeze(1).to_broadcast(whole),
                                        partf.unsqueeze(3).to_broadcast(whole), ALU.is_equal)
                dve.drain()
                nc.vector.tensor_tensor(pick, pick, bestf.unsqueeze(1).to_broadcast(whole), ALU.mult)
                dve.drain()
                nc.vector.tensor_reduce(keys, pick, mybir.AxisListType.X, ALU.add)
                dve.drain()
                nc.vector.scalar_tensor_tensor(out=idx[:, b, :], in0=keys[:, :, 0], scalar=float(NKEYS),
                                               in1=keys[:, :, 1], op0=ALU.mult, op1=ALU.add).then_inc(s_idx, 1)
                dve.drain()

            def add_y(g, b, into_new):
                dve.wait_ge(s_vu, 16 * g + 16)
                y = yps[b % 2][:, :]
                if into_new:
                    nc.vector.tensor_copy(yacc[:, b, :], y).then_inc(s_yr, 1)
                else:
                    nc.vector.tensor_tensor(yacc[:, b, :], yacc[:, b, :], y, ALU.add).then_inc(s_yr, 1)

            def dot(b, g, s):
                dve.wait_ge(s_u[s % RING], 16 * (2 * g + s // RING + 1))
                row = u_ring[:, s % RING, :]
                nc.vector.tensor_tensor_reduce(out=row, in0=row, in1=h2[:, b, :], scale=1.0, scalar=0.0,
                                               op0=ALU.mult, op1=ALU.add,
                                               accum_out=dots[:, b % 2, s:s + 1]).then_inc(s_dot, 1)

            def weights(b, g):
                dve.wait_ge(s_exp, g + 1)
                nc.vector.reciprocal(rsum, esum[:, b % 2, :])
                dve.drain()
                dve.wait_ge(s_gel, g + 1)
                nc.vector.scalar_tensor_tensor(out=coef[:, b % 2, :], in0=act_[:, b % 2, :], scalar=rsum,
                                               in1=expo[:, b % 2, :], op0=ALU.mult, op1=ALU.mult).then_inc(s_coef, 1)

            def slot(h, b, g, more=True):
                if more:
                    select(g + 1, (b + 1) % NB)
                for s in range(TOPK):
                    dot(b, g, s)
                weights(b, g)

            def finish(b):
                ln_t = ln_ts[b % 2]
                dve.wait_ge(s_x1, b + 1)
                dve.drain()
                nc.vector.tensor_tensor(ln_t, yacc[:, b, :], gate2, ALU.mult)
                dve.drain()
                nc.vector.scalar_tensor_tensor(out=ln_t, in0=x_sb[:, b, :], scalar=ALPHA, in1=ln_t,
                                               op0=ALU.mult, op1=ALU.add)
                dve.drain()
                standardise(NB + b + 1, ln_t, ln_t)
                nc.vector.tensor_tensor(ln_t, ln_t, lng, ALU.mult)
                dve.drain()
                nc.vector.tensor_tensor(x_sb[:, b, :], ln_t, lnb, ALU.add).then_inc(s_fin, 1)

            add_x(0)
            front(0)
            select(0, 0)
            add_x(1)
            front(1)
            for s in range(TOPK):
                dot(0, 0, s)
            weights(0, 0)
            add_x(2)
            add_x(3)
            select(1, 1)
            front(2)
            front(3)
            for s in range(RING):
                dot(1, 1, s)
            select(2, 2)
            for s in range(RING, TOPK):
                dot(1, 1, s)
            weights(1, 1)
            add_y(0, 0, True)
            for b in range(2, NB):
                slot(0, b, b)
                add_y(b - 1, b - 1, True)
            nc.vector.memset(yacc[:, NB - 1, :], 0.0)
            dve.drain()
            with dve.Fori(1, HEADS - 1) as h:
                for b in range(NB):
                    g = h * NB + b
                    slot(h, b, g)
                    add_y(g - 1, (b - 1) % NB, False)
            dve.wait_ge(s_ln2r, 32)
            for b in range(NB):
                g = NG - NB + b
                slot(HEADS - 1, b, g, more=b < NB - 1)
                add_y(g - 1, (b - 1) % NB, False)
                if b > 0:
                    finish(b - 1)
            add_y(NG - 1, NB - 1, False)
            finish(NB - 1)

        @block.tensor
        def _(pe):
            pe.wait_ge(s_const, 1)
            pe.wait_ge(s_par, 64)
            nc.tensor.transpose(bank[6][:, 0:26], prow[0:26, :], ident[0:26, 0:26]).then_inc(s_colps, 1)
            pe.wait_ge(s_x, 16)
            for k in range(KC):
                if k >= 2:
                    pe.wait_ge(s_xte, k - 1)
                for b in range(NB):
                    mm = nc.tensor.transpose(bank[4 + k % 2][:, b * P:(b + 1) * P], x_sb[:, b, k * P:(k + 1) * P],
                                             ident[:, :])
                mm.then_inc(s_xt, 1)
            pe.wait_ge(s_mu, KC)
            for j in range(2 * KC):
                mm = nc.tensor.matmul(bank[7][:, j:j + 1], mod_cols[:, j * P:(j + 1) * P], ones[:, 0:1],
                                      start=True, stop=True)
            mm.then_inc(s_mc, 1)

            def mod_rows():
                pe.wait_ge(s_mu, MT)
                for j in range(8):
                    if j >= 2:
                        pe.wait_ge(s_rbe, j - 1)
                    nc.tensor.matmul(bank[6 + j % 2], ones[:, :], rows[:, 2 * D + 512 * j:2 * D + 512 * (j + 1)],
                                     start=True, stop=True).then_inc(s_rb, 1)

            def gates():
                pe.wait_ge(s_wq, 16)
                pe.wait_ge(s_ja, 1)
                for i in range(GP):
                    nc.tensor.matmul(bank[4 + i], gate_up[:, i * P:(i + 1) * P], glr, start=True,
                                     stop=True).then_inc(s_z, 1)

            def project(j):
                n, kind, i = jobs[j]
                if j == first_job[n]:
                    pe.wait_ge(s_w[n % 4], 16 * (n // 4 + 1))
                if before[j] is not None:
                    e, count = read_by[before[j]]
                    pe.wait_ge(s_ja if e == "a" else s_jv, count)
                w, to = w_ring[:, n % 4], bank[job_bank[j]]
                if kind == "v":
                    for bb in range(2):
                        b = 2 * i[1] + bb
                        for k in range(KC):
                            mm = nc.tensor.matmul(to[:, WT * bb:WT * (bb + 1)], hT[:, k, b * P:(b + 1) * P],
                                                  w[:, k, :], start=k == 0, stop=k == KC - 1)
                else:
                    m = RANK if kind == "glr" else P
                    lo = 0 if kind == "glr" else P * (j - first_job[n])
                    for k in range(KC):
                        if j == 0:
                            pe.wait_ge(s_h, k + 1)
                        mm = nc.tensor.matmul(to[0:m, :], w[:, k, lo:lo + m], hT[:, k, :],
                                              start=k == 0, stop=k == KC - 1)
                mm.then_inc(s_job, 1)

            def turn_keys():
                pe.wait_ge(s_gv, 3)
                kl = gx2.rearrange("p (c t) -> p c t", c=GP)
                for i in range(GP):
                    for b in range(NB):
                        mm = nc.tensor.transpose(bank[4 + i][:, b * P:(b + 1) * P], kl[:, i, b * P:(b + 1) * P],
                                                 ident[:, :])
                    mm.then_inc(s_klp, 1)

            def chunk_kv(i):
                pe.wait_ge(s_klt, i + 1)
                if i == 0:
                    for j in range(n_attn):
                        if job_bank[j] in (2, 3) and j + 4 >= n_attn:
                            pe.wait_ge(s_ja, read_by[j][1])
                else:
                    pe.wait_ge(s_st, i)
                for n in range(NCH - 1):
                    lo = CHUNK * (n % 2)
                    for hh in range(2):
                        hd = 2 * i + hh
                        col = 512 * (n % 2) + P * (n // 2)
                        mm = nc.tensor.matmul(pb[DK * hh:DK * (hh + 1), col:col + P],
                                              klT[lo:lo + CHUNK, i, n // 2, DK * hh:DK * (hh + 1)],
                                              v_[lo:lo + CHUNK, n // 2, hd * P:(hd + 1) * P], start=True, stop=True)
                mm.then_inc(s_kv, 1)

            def scores_of(hd):
                i, lo = hd // 2, DK * (hd % 2)
                if hd >= 2:
                    pe.wait_ge(s_am, hd - 1)
                for b in range(NB):
                    mm = nc.tensor.matmul(bank[6 + hd % 2][:, b * P:(b + 1) * P],
                                          k_[lo:lo + DK, i, b * P:(b + 1) * P],
                                          q_[lo:lo + DK, i, b * P:(b + 1) * P], start=True, stop=True)
                mm.then_inc(s_at, 1)

            def outputs_of(hd):
                i, lo = hd // 2, DK * (hd % 2)
                pe.wait_ge(s_am, hd + 1)
                pe.wait_ge(s_st, i + 1)
                if hd >= 2:
                    pe.wait_ge(s_mix, hd - 1)
                o = bank[4 + hd % 2]
                for b in range(NB):
                    mm = nc.tensor.matmul(o[:, b * P:(b + 1) * P], v_[:, b, hd * P:(hd + 1) * P],
                                          attn[:, hd % 2, b, :], start=True, stop=False, skip_group_check=True)
                    for n in (2 * b, 2 * b + 1):
                        if n == 0:
                            continue
                        mm = nc.tensor.matmul(o[:, n * CHUNK:(n + 1) * CHUNK], state[i][lo:lo + DK, n - 1, :],
                                              q_[lo:lo + DK, i, n * CHUNK:(n + 1) * CHUNK],
                                              start=False, stop=n % 2 == 1, skip_group_check=True)
                mm.then_inc(s_o, 1)

            def mean_square(hd):
                pe.wait_ge(s_sq, hd + 1)
                if hd < 2:
                    pe.wait_ge(s_st, GP)
                else:
                    pe.wait_ge(s_msv, hd - 1)
                nc.tensor.matmul(bank[2 + hd % 2], ones[:, :], sq[:, hd % 2, :], start=True, stop=True).then_inc(s_ms, 1)

            for j in range(n_attn):
                project(j)
                if j == 2:
                    gates()
            mod_rows()
            conv = n_attn
            project(conv)
            turn_keys()
            project(conv + 1)
            chunk_kv(0)
            project(conv + 2)
            chunk_kv(1)
            pe.wait_ge(s_gv, 4)
            pe.wait_ge(s_rbe, 8)
            scores_of(0)
            scores_of(1)
            project(conv + 3)
            outputs_of(0)
            scores_of(2)
            project(conv + 4)
            outputs_of(1)
            mean_square(0)
            scores_of(3)
            project(conv + 5)
            mean_square(1)
            outputs_of(2)
            project(conv + 6)
            mean_square(2)
            outputs_of(3)
            project(conv + 7)
            mean_square(3)
            for j in range(conv + 8, conv + 12):
                project(j)

            def scores(g, b):
                if not (isinstance(g, int) and g < 2):
                    pe.wait_ge(s_scr, g - 1)
                for p in range(2):
                    mm = nc.tensor.matmul(sps[b % 2][:, p, :], qT[:, p, b * P:(b + 1) * P], skT[:, p, :],
                                          start=True, stop=True)
                mm.then_inc(s_sc, 1)

            def subkeys(h):
                pe.wait_ge(s_wq, 16 * (2 * h + 3))
                for p in range(2):
                    mm = nc.tensor.transpose(pc[:, NKEYS * p:NKEYS * (p + 1)], sk_sb[:, p, :], ident[:, :])
                mm.then_inc(s_skp, 1)

            def mix(b, halves=(0, 1)):
                if b >= 2:
                    pe.wait_ge(s_lnz, b - 1)
                for half in halves:
                    for n, k in enumerate([*range(CC, KC), *range(CC)]):
                        if b == 0 and half == 0 and n == 0:
                            pe.wait_ge(s_mix, GH)
                            pe.wait_ge(s_jv, counts["v"] - 2)
                        if b == 0 and half == 0 and n == KC - 2:
                            pe.wait_ge(s_jv, counts["v"])
                        if b == 0 and half == 0:
                            pe.wait_ge(s_wg, k + 1)
                        mm = nc.tensor.matmul(yps[(b + 1) % 2][:, 512 * half:512 * (half + 1)], mixT[:, k, b * P:(b + 1) * P],
                                              wout[:, k, 512 * half:512 * (half + 1)], start=n == 0, stop=n == KC - 1)
                if 1 in halves:
                    mm.then_inc(s_wop, 1)

            def front(b):
                pe.wait_ge(s_h2, b + 1)
                if b > 0:
                    pe.wait_ge(s_qe, b)
                for k in range(KC):
                    mm = nc.tensor.transpose(pc[:, k * P:(k + 1) * P], h2[:, b, k * P:(k + 1) * P], ident[:, :])
                mm.then_inc(s_tp, 1)
                pe.wait_ge(s_tpe, b + 1)
                for p in range(2):
                    for k in range(KC):
                        mm = nc.tensor.matmul(pc[:, 512 * p:512 * p + P], wq_sb[:, k, p * P:(p + 1) * P],
                                              hT[:, k, b * P:(b + 1) * P], start=k == 0, stop=k == KC - 1)
                mm.then_inc(s_qp, 1)
                pe.wait_ge(s_qe, b + 1)
                scores(b, b)

            def next_query(h, p):
                if p == 0:
                    pe.wait_ge(s_wq, 16 * (2 * h + 3))
                    pe.wait_ge(s_ske, h)
                for k in range(KC):
                    mm = nc.tensor.matmul(pc[:, 512 * p:512 * (p + 1)], wq_sb[:, k, p * P:(p + 1) * P],
                                          hT[:, k, :], start=k == 0, stop=k == KC - 1)
                if p == 1:
                    mm.then_inc(s_qp, 1)
                    pe.wait_ge(s_qe, NB + h)
                    subkeys(h)

            def weigh(g, b, experts=range(TOPK)):
                if not (isinstance(g, int) and g < 2):
                    pe.wait_ge(s_yr, g - 1)
                for s in experts:
                    pe.wait_ge(s_diag, 16 * g + s + 1)
                    pe.wait_ge(s_v[s % RING], 16 * (2 * g + s // RING + 1))
                    for half in range(2):
                        mm = nc.tensor.matmul(yps[b % 2][:, 512 * half:512 * (half + 1)], diag[:, s, :],
                                              v_ring[:, s % RING, 512 * half:512 * (half + 1)],
                                              start=s == 0, stop=s == TOPK - 1)
                    mm.then_inc(s_vu, 1)

            mix(0)
            subkeys(0)
            mix(1, halves=(0,))
            pe.wait_ge(s_ske, 1)
            front(0)
            mix(1, halves=(1,))
            mix(2)
            mix(3)
            front(1)
            pe.wait_ge(s_lnz, NB)
            weigh(0, 0, range(RING))
            front(2)
            front(3)
            weigh(0, 0, range(RING, TOPK))
            next_query(1, 0)
            next_query(1, 1)
            for b in range(2, NB):
                if b == 2:
                    pe.wait_ge(s_ske, 2)
                scores(b + 2, (b + 2) % NB)
                weigh(b - 1, b - 1)
            with pe.Fori(1, HEADS - 1) as h:
                for b in range(NB):
                    g = h * NB + b
                    if b == 2:
                        pe.wait_ge(s_ske, h + 2)
                    scores(g + 2, (b + 2) % NB)
                    weigh(g - 1, (b - 1) % NB)
                    if b < 2:
                        next_query(h + 1, b)
            for b in range(NB):
                g = NG - NB + b
                if b < 2:
                    scores(g + 2, b + 2)
                weigh(g - 1, (b - 1) % NB)
            weigh(NG - 1, NB - 1)


_INS = ["x", "c", "w_mod", "b_mod", "w_in", "conv_w", "gla_gate_up", "gla_gate_bias", "gla_norm_g", "w_out",
        "ln1_g", "ln1_b", "peer_wq", "peer_subkeys", "peer_u", "peer_v", "ln2_g", "ln2_b"]


def kernel(**inputs):
    import numpy as np
    import concourse.bacc as bacc
    from concourse.bass_utils import run_bass_kernel_spmd

    nc = bacc.Bacc("TRN2", target_bir_lowering=False, num_devices=1)
    arrays, args = {}, []
    for name in _INS:
        a = np.ascontiguousarray(inputs[name])
        arrays[f"in_{name}"] = a
        args.append(nc.dram_tensor(f"in_{name}", a.shape, mybir.dt.from_np(a.dtype), kind="ExternalInput").ap())
    args.append(nc.dram_tensor("out_0", inputs["x"].shape, F32, kind="ExternalOutput").ap())
    build(nc, *args)
    r = run_bass_kernel_spmd(nc, [arrays], core_ids=[0])
    return r.results[0]["out_0"]
```

```python
from contextlib import ExitStack

import concourse.bass as bass
from concourse import mybir

F32 = mybir.dt.float32
U32 = mybir.dt.uint32
ALU = mybir.AluOpType
ACT = mybir.ActivationFunctionType

P = 128
LN_EPS = 1e-5
RMS_EPS = 1e-6
GLA_TAU = 16.0
CHUNK = 64
TOPK = 16
RING = 8
STEP = 2
LOWEST = -3.0e38


def build(nc, x, c, w_mod, b_mod, w_in, conv_w, gla_gate_up, gla_gate_bias, gla_norm_g, w_out,
          ln1_g, ln1_b, peer_wq, peer_subkeys, peer_u, peer_v, ln2_g, ln2_b, out):
    _, SEQ, D = x.shape
    KC = D // P
    NB = SEQ // P
    CW = conv_w.shape[1]
    CC = CW // P
    RANK, GK = gla_gate_up.shape
    GV = gla_norm_g.shape[0]
    GH = GV // P
    GP = GK // P
    DK = GK // GH
    NCH = SEQ // CHUNK
    HEADS, _, NKEYS, HALF = peer_subkeys.shape
    QD = 2 * HALF
    NG = HEADS * NB
    ALPHA = 2.0 ** 0.25
    assert NB == 4 and HALF == P and NKEYS == P

    ctx = ExitStack()
    with ctx:
        def sb(name, shape, dt=F32):
            return ctx.enter_context(nc.sbuf_tensor(name, shape, dt))

        def psum(name):
            return ctx.enter_context(nc.psum_tensor(name, [P, 1024], F32))

        def sem(name):
            return ctx.enter_context(nc.semaphore(name))

        u_ring = sb("u_ring", [P, RING, D])
        v_ring = sb("v_ring", [P, RING, D])
        x_sb = sb("x_sb", [P, NB, D])
        hT = sb("hT", [P, KC, SEQ])
        h2 = sb("h2", [P, NB, D])
        mixT = sb("mixT", [P, KC, SEQ])
        rows = sb("rows", [P, 6 * D])
        mid = sb("mid", [P, 6656])
        gx = sb("gx", [P, 3 * 1024])
        wq_sb = sb("wq_sb", [P, KC, QD])
        misc = sb("misc", [P, 2 * SEQ])
        ident = sb("ident", [P, P])
        ones = sb("ones", [P, P])
        causal = sb("causal", [P, P])
        prow = sb("prow", [32, P])
        pcol = sb("pcol", [P, 32])
        siluc = sb("siluc", [P, KC])
        modc = sb("modc", [P, 2 * KC])
        gate_up = sb("gate_up", [RANK, GK])

        w_ring = u_ring[:, :, :].rearrange("p a b -> p (a b)").rearrange("p (s k c) -> p s k c", s=4, k=KC)
        m_ring = v_ring[:, :, :].rearrange("p a b -> p (a b)").rearrange("p (s c) -> p s c", s=4)
        wout = v_ring
        h2f = h2[:, :, :].rearrange("p a b -> p (a b)")
        cgate = h2f[:, 0:CC * SEQ].rearrange("p (c t) -> p c t", c=CC)
        uconv = h2f[:, CC * SEQ:2 * CC * SEQ].rearrange("p (c t) -> p c t", c=CC)
        q_ = mid[:, 0:1024].rearrange("p (c t) -> p c t", c=GP)
        k_ = mid[:, 1024:2048].rearrange("p (c t) -> p c t", c=GP)
        v_ = mid[:, 2048:4096].rearrange("p (b e) -> p b e", b=NB)
        r_ = mid[:, 4096:6144].rearrange("p (h t) -> p h t", h=GH)
        glr = mid[0:RANK, 6144:6656]
        gx0, gx1, gx2 = (gx[:, 1024 * i:1024 * (i + 1)] for i in range(3))
        restart = misc[:, SEQ:2 * SEQ]
        attn = misc[:, :].rearrange("p (i b t) -> p i b t", i=2, b=NB)
        wqf = wq_sb[:, :, :].rearrange("p k c -> p (k c)")
        klT = wqf[:, 0:1024].rearrange("p (c b d) -> p c b d", c=GP, b=NB)
        state = [wqf[:, o:o + (NCH - 1) * P].rearrange("p (n e) -> p n e", e=P) for o in (1024, 0)]
        sq = gx1.rearrange("p (i t) -> p i t", i=2)
        rms = gx2.rearrange("p (i t) -> p i t", i=2)

        diag = mid[:, 0:2048].rearrange("p (s t) -> p s t", s=TOPK)
        ln_ts = [mid[:, 2048:3072], mid[:, 5120:6144]]
        fold_tmp = mixT[:, KC - 2:KC, :].rearrange("p k t -> p (k t)")
        ln2g = mid[:, 3072:4096]
        qT = mid[:, 4096:5120].rearrange("p (a t) -> p a t", a=2)
        sk_sb = misc[:, 0:2 * HALF].rearrange("p (a n) -> p a n", a=2)
        skT = misc[:, 2 * HALF:4 * HALF].rearrange("p (a n) -> p a n", a=2)
        yacc = mixT[:, :, :].rearrange("p a b -> p (a b)").rearrange("p (b d) -> p b d", b=NB)
        at = [0]

        def small(shape, dt=F32):
            n = 1
            for s in shape:
                n *= s
            v = gx[:, at[0]:at[0] + n]
            at[0] += n
            if dt is not F32:
                v = v.bitcast(dt)
            if len(shape) == 2:
                v = v.rearrange("p (a b) -> p a b", a=shape[0])
            if len(shape) == 3:
                v = v.rearrange("p (a b c) -> p a b c", a=shape[0], b=shape[1])
            return v

        rest = small([2, NKEYS])
        best = small([2, TOPK])
        besti = small([2, TOPK], U32)
        bestf = small([2, TOPK])
        cand = small([TOPK, TOPK])
        cand2 = small([TOPK, TOPK])
        pos = small([TOPK], U32)
        part = small([TOPK, 2], U32)
        partf = small([TOPK, 2])
        pick = small([TOPK, 2, TOPK])
        keys = small([TOPK, 2])
        top = small([2, TOPK])
        ntop = small([2, 1])
        expo = small([2, TOPK])
        esum = small([2, 1])
        rsum = small([1])
        dots = small([2, TOPK])
        act_ = small([2, TOPK])
        coef = small([2, TOPK])
        stats = small([2, 6])
        mv = small([2])
        std = small([1])
        rstd = small([1])
        seq16 = sb("seq16", [P, TOPK])
        idx = sb("idx", [P, NB, TOPK], U32)

        mod_cols = rows[:, 0:2 * D]
        lng, lnb = rows[:, 0:D], rows[:, D:2 * D]
        gate1, shift2, scale2, gate2 = (rows[:, D * i:D * (i + 1)] for i in (2, 3, 4, 5))

        ln2b = gate1

        pa, pb, pc, pd = psum("pa"), psum("pb"), psum("pc"), psum("pd")
        bank = [t[:, 512 * i:512 * (i + 1)] for t in (pa, pb, pc, pd) for i in range(2)]
        yps = [pa, pb]
        sps = [pd[:, 512 * i:512 * i + 256].rearrange("p (a n) -> p a n", a=2) for i in range(2)]

        s_par = sem("params_landed")
        s_bmod = sem("b_mod_landed")
        s_x = sem("x_landed")
        s_m = [sem(f"w_mod_landed{i}") for i in range(4)]
        s_w = [sem(f"w_in_landed{i}") for i in range(4)]
        s_lnr = sem("ln_rows_landed")
        s_ln2r = sem("ln2_rows_landed")
        s_wo = sem("w_out_landed")
        s_wq = sem("wq_landed")
        s_u = [sem(f"u_landed{i}") for i in range(RING)]
        s_v = [sem(f"v_landed{i}") for i in range(RING)]
        s_out = sem("out_stored")
        s_const = sem("constants_made")
        s_zero = sem("rows_zeroed")
        s_colps = sem("param_columns_in_psum")
        s_col = sem("param_columns_ready")
        s_xt = sem("x_transposed")
        s_xte = sem("x_transposes_copied")
        s_mu = sem("w_mod_tile_used")
        s_mc = sem("mod_columns_in_psum")
        s_mce = sem("mod_columns_ready")
        s_h = sem("hT_ready")
        s_job = sem("projection_in_psum")
        s_ja = sem("projection_copied_by_scalar")
        s_jv = sem("projection_read_by_vector")
        s_rb = sem("mod_rows_in_psum")
        s_rbe = sem("mod_rows_ready")
        s_z = sem("gate_in_psum")
        s_gs = sem("gate_step_of_scalar")
        s_gv = sem("gate_step_of_vector")
        s_klp = sem("klT_in_psum")
        s_klt = sem("klT_ready")
        s_kv = sem("kv_in_psum")
        s_st = sem("state_ready")
        s_at = sem("scores_of_attention_in_psum")
        s_am = sem("attention_masked")
        s_o = sem("o_in_psum")
        s_sq = sem("o_squared")
        s_ms = sem("mean_square_in_psum")
        s_msv = sem("mean_square_read")
        s_rt = sem("rms_root_ready")
        s_mix = sem("mix_ready")
        s_wg = sem("w_out_rows_gated")
        s_fold = sem("h2_rows_folded")
        s_x1g = sem("x1_product_ready")
        s_x1 = sem("x1_ready")
        s_wop = sem("w_out_product_in_psum")
        s_lv = sem("ln_variance_ready")
        s_ls = sem("ln_std_ready")
        s_lnz = sem("w_out_product_read")
        s_h2 = sem("h2_ready")
        s_tp = sem("h2_transposed")
        s_tpe = sem("h2T_ready")
        s_skp = sem("subkeys_transposed")
        s_ske = sem("subkeysT_ready")
        s_qp = sem("query_in_psum")
        s_qe = sem("query_ready")
        s_sc = sem("scores_in_psum")
        s_scr = sem("scores_read")
        s_top = sem("top_ready")
        s_exp = sem("exp_ready")
        s_idx = sem("idx_ready")
        s_dot = sem("dot_done")
        s_gel = sem("gelu_ready")
        s_coef = sem("coef_ready")
        s_diag = sem("diag_ready")
        s_vu = sem("v_rows_used")
        s_yr = sem("y_read")
        s_fin = sem("result_ready")

        WT = 256
        tiles = [12, 6, 7, 8, 9, 10, 11, 2, 4, 0, 3, 5, 1]
        q_tile, k_tile, v_tile, r_tile, g_tile = 6, 7, 8, 10, 12
        HALF_SEQ = SEQ // 2
        jobs, later = [], []
        for n, t in enumerate(tiles):
            if t == g_tile:
                jobs.append((n, "glr", 0, 0, 0, SEQ))
            elif v_tile <= t < v_tile + 2:
                jobs += [(n, "v", (t - v_tile, i), i, 0, SEQ) for i in range(2)]
            elif n < len(tiles) - 4:
                kind, first = {q_tile: ("q", 0), k_tile: ("k", 0), r_tile: ("r", 0), r_tile + 1: ("r", 2)}.get(
                    t, (("cb", "cc", "ch")[t // 2 % 3], 2 * (t % 2)))
                jobs += [(n, kind, first + i, i, 0, SEQ) for i in range(2)]
            else:
                kind = ("cb", "cc", "ch")[t // 2]
                jobs += [(n, kind, 2 * (t % 2) + i, i, 0, HALF_SEQ) for i in range(2)]
                later += [(n, kind, 2 * (t % 2) + i, i, HALF_SEQ, SEQ) for i in range(2)]
        n_first = len(jobs)
        jobs += later
        by_vector = ("cb", "ch")
        read_by, counts = [], {"a": 0, "v": 0}
        for job in jobs:
            e = "v" if job[1] in by_vector else "a"
            counts[e] += 1
            read_by.append((e, counts[e]))
        n_attn = sum(job[1] not in ("cb", "cc", "ch") for job in jobs)
        job_bank = [j % 4 if j < n_attn else (j - n_attn) % 2 if j < n_first else (j - n_first) % (4 if j < n_first + 6 else 2)
                    for j in range(len(jobs))]
        before = [max((m for m in range(j) if job_bank[m] == job_bank[j]), default=None) for j in range(len(jobs))]
        first_job = [min(j for j, job in enumerate(jobs) if job[0] == n) for n in range(len(tiles))]
        last_job = [max(j for j, job in enumerate(jobs) if job[0] == n) for n in range(len(tiles))]

        def w_slot(n):
            return (n - len(tiles)) % 4

        def used_up(i):
            return n_first + 2 * i + 2

        MT = 3 * KC

        def mod_tile(i):
            return (i, 0) if i < KC else ((i - KC) // 2, 2 * D * (1 + (i - KC) % 2))

        def mix_ps(b):
            return pa if b == 2 else pb

        def rows_bank(j):
            return bank[(6 if j < 6 else 4) + j % 2]

        block = ctx.enter_context(nc.Block())

        @block.sync
        def _(sp):
            sp.dma_start(prow[0:8, :], c.rearrange("a (k p) -> (a k) p", p=P)).then_inc(s_par, 16)
            sp.dma_start(prow[8:10, :], gla_gate_bias.rearrange("(k p) -> k p", p=P)).then_inc(s_par, 16)
            sp.dma_start(prow[10:14, :], gla_norm_g.rearrange("(k p) -> k p", p=P)).then_inc(s_par, 16)
            sp.dma_start(prow[14:26, :], conv_w.rearrange("j (k p) -> (j k) p", p=P)).then_inc(s_par, 16)

            def load_mod(i):
                k, col = mod_tile(i)
                if i >= 4:
                    sp.wait_ge(s_mu, i - 3)
                sp.dma_start(m_ring[:, i % 4, :], w_mod[k * P:(k + 1) * P, col:col + 2 * D]).then_inc(s_m[i % 4], 16)

            def load_win(n):
                if n >= 4:
                    sp.wait_ge(s_job, last_job[n - 4] + 1)
                col = WT * tiles[n]
                width = min(WT, w_in.shape[1] - col)
                sp.dma_start(w_ring[:, w_slot(n), :, 0:width],
                             w_in[:, col:col + width].rearrange("(k p) c -> p k c", p=P)).then_inc(s_w[w_slot(n)], 16)

            for i in range(4):
                load_mod(i)
            sp.wait_ge(s_zero, 1)
            sp.dma_start(rows[0:1, :], b_mod.rearrange("(a n) -> a n", a=1)).then_inc(s_bmod, 16)
            sp.dma_start(x_sb[:, :, :], x[0].rearrange("(b p) d -> p b d", p=P)).then_inc(s_x, 16)
            for i in range(4, KC):
                load_mod(i)
            sp.dma_start(gate_up[:, :], gla_gate_up).then_inc(s_wq, 16)
            for n in range(4):
                load_win(n)
            i = KC
            for n in range(4, len(tiles)):
                for _ in range(6 if n == 4 else 4):
                    if i < MT:
                        load_mod(i)
                        i += 1
                load_win(n)
                if n == 7:
                    sp.wait_ge(s_mce, 2)
                    sp.dma_start(lng, ln1_g.partition_broadcast(P)).then_inc(s_lnr, 16)
                    sp.dma_start(lnb, ln1_b.partition_broadcast(P)).then_inc(s_lnr, 16)
                if n == 9:
                    sp.wait_ge(s_mu, MT)
                    sp.dma_start(wout[:, :, :], w_out.rearrange("(k p) n -> p k n", p=P)).then_inc(s_wo, 16)
            sp.wait_ge(s_o, GH)
            sp.dma_start(wq_sb[:, :, :], peer_wq[:, 0:QD].rearrange("(k p) c -> p k c", p=P)).then_inc(s_wq, 16)
            sp.dma_start(sk_sb, peer_subkeys[0].rearrange("a n d -> n a d")).then_inc(s_wq, 16)
            sp.dma_start(ln2g, ln2_g.partition_broadcast(P)).then_inc(s_ln2r, 16)
            sp.wait_ge(s_wg, KC)
            sp.dma_start(ln2b, ln2_b.partition_broadcast(P)).then_inc(s_ln2r, 16)
            sp.wait_ge(s_qe, NB)
            with sp.Fori(1, HEADS) as h:
                sp.wait_ge(s_ske, h)
                sp.dma_start(wq_sb[:, :, :], peer_wq[:, bass.ds(h * QD, QD)].rearrange("(k p) c -> p k c", p=P)).then_inc(s_wq, 16)
                sp.dma_start(sk_sb, peer_subkeys[bass.ds(h, 1)].rearrange("o a n d -> n (o a) d")).then_inc(s_wq, 16)
            for b in range(NB):
                for half in range(2):
                    cols = slice(D // 2 * half, D // 2 * (half + 1))
                    sp.wait_ge(s_fin, 2 * b + half + 1)
                    sp.dma_start(out[0, b * P:(b + 1) * P, cols], x_sb[:, b, cols]).then_inc(s_out, 16)
            sp.wait_ge(s_out, 16 * 2 * NB)

        @block.gpsimd
        def _(pool):
            nc.gpsimd.memset(rows[:, :], 0.0).then_inc(s_zero, 1)
            nc.gpsimd.memset(ident[:, :], 0.0)
            nc.gpsimd.memset(ones[:, :], 1.0)
            nc.gpsimd.memset(causal[:, :], 1.0)
            nc.gpsimd.memset(restart, 1.0)
            nc.gpsimd.iota(seq16[:, :], [[1, TOPK]], base=0, channel_multiplier=0,
                           allow_small_or_imprecise_dtypes=True)
            pool.drain()
            nc.gpsimd.affine_select(out=ident[:, :], in_=ident[:, :], compare_op=ALU.not_equal, fill=1.0,
                                    base=0, pattern=[[-1, P]], channel_multiplier=1)
            nc.gpsimd.affine_select(out=causal[:, :], in_=causal[:, :], compare_op=ALU.is_ge, fill=0.0,
                                    base=0, pattern=[[1, P]], channel_multiplier=-1)
            nc.gpsimd.memset(restart.rearrange("p (n t) -> p n t", t=CHUNK)[:, :, 0:1], 0.0)
            pool.drain()
            nc.gpsimd.memset(causal[0:CHUNK, CHUNK:P], 0.0).then_inc(s_const, 1)

            def gather(ring, table, idx_col, landed):
                pool.indirect_dma_start(ring, None, table[:, :],
                                        bass.IndirectOffsetOnAxis(ap=idx_col, axis=0)).then_inc(landed, 16)

            def gather_u(b, s):
                gather(u_ring[:, s % RING, :], peer_u, idx[:, b, s:s + 1], s_u[s % RING])

            def gather_v(b, s):
                gather(v_ring[:, s % RING, :], peer_v, idx[:, b, s:s + 1], s_v[s % RING])

            def x1(b, half):
                if half == 0:
                    pool.wait_ge(s_h2, b + 1)
                    nc.gpsimd.tensor_tensor(x_sb[:, b, :], x_sb[:, b, :], lng, ALU.mult).then_inc(s_x1g, 1)
                else:
                    pool.wait_ge(s_x1g, b + 1)
                    nc.gpsimd.tensor_tensor(x_sb[:, b, :], x_sb[:, b, :], lnb, ALU.add).then_inc(s_x1, 1)

            def slot(h, b, g, u=True, v=True, x1_blocks=()):
                first = isinstance(g, int) and g == 0
                if u:
                    pool.wait_ge(s_idx, g + 1)
                    pool.nop(nofuse=True)
                for s in range(TOPK):
                    if first and s < RING and s % 2 == 0:
                        pool.wait_ge(s_job, used_up(s // 2))
                        pool.nop(nofuse=True)
                    if u and s % STEP == 0 and not (first and s < RING):
                        pool.wait_ge(s_dot, 16 * g + s + STEP - RING)
                        pool.nop(nofuse=True)
                    if u:
                        gather_u(b, s)
                    if v and s % STEP == 0:
                        pool.wait_ge(s_vu, 16 * (g - 1) + s + STEP - RING)
                        pool.nop(nofuse=True)
                    if v:
                        gather_v((b - 1) % NB, s)
                    if x1_blocks and s % 4 == 3:
                        x1(x1_blocks[s // 8], s // 4 % 2)

            def times(dst, a, b):
                return nc.gpsimd.tensor_tensor(dst, a, b, ALU.mult)

            def plus(dst, a, b):
                return nc.gpsimd.tensor_tensor(dst, a, b, ALU.add)

            pool.wait_ge(s_rbe, 6)
            pool.wait_ge(s_lnr, 32)
            times(fold_tmp, lnb, scale2)
            pool.drain()
            plus(shift2, shift2, fold_tmp)
            times(scale2, scale2, lng).then_inc(s_fold, 1)
            pool.wait_ge(s_wo, 16)
            for k in range(KC):
                times(wout[:, k, :], wout[:, k, :], gate1).then_inc(s_wg, 1)

            slot(0, 0, 0, v=False)
            pool.wait_ge(s_idx, 2)
            pool.nop(nofuse=True)

            def u1(s):
                if s % STEP == 0:
                    pool.wait_ge(s_dot, 16 + s + STEP - RING)
                    pool.nop(nofuse=True)
                gather_u(1, s)

            for s in range(TOPK - RING // 2):
                u1(s)
            pool.wait_ge(s_wop, NB)
            pool.nop(nofuse=True)
            for s in range(RING):
                gather_v(0, s)
            for s in range(RING):
                if s % 2 == 0:
                    u1(TOPK - RING // 2 + s // 2)
                if s % STEP == 0:
                    pool.wait_ge(s_vu, s + STEP)
                    pool.nop(nofuse=True)
                gather_v(0, s + RING)
            for b in range(2, NB):
                slot(0, b, b, x1_blocks=(2 * b - 4, 2 * b - 3))
            with pool.Fori(1, HEADS) as h:
                for b in range(NB):
                    slot(h, b, h * NB + b)
            slot(HEADS, 0, NG, u=False)

        @block.scalar
        def _(act):
            def copy(dst, src):
                return nc.scalar.activation(dst, src, ACT.Copy)

            act.wait_ge(s_colps, 1)
            copy(pcol[:, 0:26], bank[6][:, 0:26])
            act.drain()
            nc.scalar.activation(siluc[:, :], pcol[:, 0:KC], ACT.Silu).then_inc(s_col, 1)
            for k in range(KC):
                act.wait_ge(s_xt, k + 1)
                copy(hT[:, k, :], bank[4 + k % 2]).then_inc(s_xte, 1)
            for part in range(2):
                lo, hi = KC * part // 2, KC * (part + 1) // 2
                act.wait_ge(s_mc, part + 1)
                copy(modc[:, lo:hi], bank[7 - part][:, lo:hi])
                nc.scalar.activation(modc[:, KC + lo:KC + hi], bank[7 - part][:, KC + lo:KC + hi],
                                     ACT.Identity, bias=1.0).then_inc(s_mce, 1)
                act.drain()
                for k in range(lo, hi):
                    nc.scalar.activation(hT[:, k, :], hT[:, k, :], ACT.Identity, bias=modc[:, k:k + 1],
                                         scale=modc[:, KC + k:KC + k + 1]).then_inc(s_h, 1)

            def mod_rows(steps):
                for j in steps:
                    act.wait_ge(s_rb, j + 1)
                    plus = 0.0 if j // 2 == 1 else 1.0
                    nc.scalar.activation(rows[:, 2 * D + 512 * j:2 * D + 512 * (j + 1)], rows_bank(j),
                                         ACT.Identity, bias=plus).then_inc(s_rbe, 1)

            def gate_logs():
                zz = gx0.rearrange("p (c t) -> p c t", c=GP)
                for i in range(GP):
                    act.wait_ge(s_z, i + 1)
                    nc.scalar.activation(zz[:, i, :], bank[4 + i], ACT.Identity, bias=pcol[:, 8 + i:9 + i])
                act.drain()
                nc.scalar.activation(gx1, gx0, ACT.Abs)
                act.drain()
                nc.scalar.activation(gx1, gx1, ACT.Exp, scale=-1.0)
                act.drain()
                nc.scalar.activation(gx1, gx1, ACT.Ln, bias=1.0).then_inc(s_gs, 1)

            def gate_exps():
                act.wait_ge(s_gv, 1)
                nc.scalar.activation(gx0, gx1, ACT.Exp, scale=1.0 / GLA_TAU).then_inc(s_gs, 1)
                act.wait_ge(s_gv, 2)
                nc.scalar.activation(gx2, gx2, ACT.Exp, scale=1.0 / GLA_TAU).then_inc(s_gs, 1)
                nc.scalar.activation(gx1, gx1, ACT.Exp, scale=-1.0 / GLA_TAU).then_inc(s_gs, 1)

            def copy_job(j):
                _, kind, i, _, lo, hi = jobs[j]
                act.wait_ge(s_job, j + 1)
                src = bank[job_bank[j]]
                if kind == "glr":
                    copy(glr, src[0:RANK, :]).then_inc(s_ja, 1)
                elif kind == "q":
                    copy(q_[:, i, :], src).then_inc(s_ja, 1)
                elif kind == "k":
                    copy(k_[:, i, :], src).then_inc(s_ja, 1)
                elif kind == "v":
                    copy(v_[:, 2 * i[1]:2 * i[1] + 2, WT * i[0]:WT * (i[0] + 1)],
                         src.rearrange("p (b e) -> p b e", b=2)).then_inc(s_ja, 1)
                elif kind == "r":
                    nc.scalar.activation(r_[:, i, :], src, ACT.Silu).then_inc(s_ja, 1)
                else:
                    copy(cgate[:, i, lo:hi], src[:, 0:hi - lo]).then_inc(s_ja, 1)

            def square(hd):
                act.wait_ge(s_o, hd + 1)
                nc.scalar.activation(sq[:, hd % 2, :], bank[4 + hd % 2], ACT.Square).then_inc(s_sq, 1)

            def root(hd):
                act.wait_ge(s_msv, hd + 1)
                nc.scalar.activation(rms[:, hd % 2, :], rms[:, hd % 2, :], ACT.Sqrt).then_inc(s_rt, 1)

            for j in range(n_attn):
                copy_job(j)
                if j == 2:
                    gate_logs()
                if j == n_attn - 3:
                    gate_exps()
            mod_rows(range(6))
            conv = n_attn
            copy_job(conv)
            for i in range(GP):
                act.wait_ge(s_klp, i + 1)
                copy(klT[:, i].rearrange("p b d -> p (b d)"), bank[4 + i]).then_inc(s_klt, 1)
            copy_job(conv + 1)
            square(0)
            square(1)
            root(0)
            copy_job(conv + 6)
            copy_job(conv + 7)
            root(1)
            square(2)
            root(2)
            square(3)
            root(3)

            def ln_root(n):
                act.wait_ge(s_lv, n)
                nc.scalar.activation(std, mv[:, 1:2], ACT.Sqrt).then_inc(s_ls, 1)

            def copy_subkeys(h):
                act.wait_ge(s_skp, h + 1)
                copy(skT[:, :, :].rearrange("p a n -> p (a n)"), pc[:, 0:2 * NKEYS]).then_inc(s_ske, 1)

            def turned(b):
                act.wait_ge(s_tp, b + 1)
                copy(hT[:, :, b * P:(b + 1) * P],
                     pc[:, :].rearrange("p (k t) -> p k t", k=KC)).then_inc(s_tpe, 1)

            def query(b):
                act.wait_ge(s_qp, b + 1)
                copy(qT[:, :, b * P:(b + 1) * P],
                     pc[:, :].rearrange("p (a t) -> p a t", a=2)[:, :, 0:P]).then_inc(s_qe, 1)

            def softmax_top(g, par):
                act.wait_ge(s_top, g + 1)
                nc.scalar.activation(expo[:, par, :], top[:, par, :], ACT.Exp, bias=ntop[:, par, :],
                                     accum_out=esum[:, par, :]).then_inc(s_exp, 1)

            def gelu(b, g):
                act.wait_ge(s_dot, 16 * g + 16)
                nc.scalar.activation(act_[:, b % 2, :], dots[:, b % 2, :], ACT.Gelu).then_inc(s_gel, 1)

            def diagonals(b, g):
                act.wait_ge(s_coef, g + 1)
                first = isinstance(g, int) and g == 0
                for s in range(TOPK):
                    if not first:
                        act.wait_ge(s_vu, 16 * (g - 1) + s + 1)
                    nc.scalar.activation(diag[:, s, :], ident[:, :], ACT.Copy,
                                         scale=coef[:, b % 2, s:s + 1]).then_inc(s_diag, 1)

            def slot(b, g, more=True):
                if more:
                    softmax_top(g + 1, (b + 1) % 2)
                gelu(b, g)
                diagonals(b, g)

            def next_head(h):
                act.wait_ge(s_qp, NB + h)
                copy(qT[:, :, :].rearrange("p a t -> p (a t)"), pc[:, :]).then_inc(s_qe, 1)
                copy_subkeys(h)

            copy_subkeys(0)
            ln_root(1)
            turned(0)
            copy_job(n_first + 2)
            query(0)
            copy_job(n_first + 3)
            softmax_top(0, 0)
            ln_root(2)
            turned(1)
            query(1)
            softmax_top(1, 1)
            gelu(0, 0)
            diagonals(0, 0)
            ln_root(3)
            turned(2)
            query(2)
            ln_root(4)
            turned(3)
            query(3)
            mod_rows(range(6, 8))
            for b in range(1, NB):
                slot(b, b)
                if b == 1:
                    next_head(1)
            with act.Fori(1, HEADS - 1) as h:
                for b in range(NB):
                    slot(b, h * NB + b)
                    if b == 1:
                        next_head(h + 1)
            for b in range(NB):
                slot(b, NG - NB + b, more=b < NB - 1)
                if b > 0:
                    ln_root(NB + b)
            ln_root(2 * NB)

        @block.vector
        def _(dve):
            dve.wait_ge(s_col, 1)
            dve.wait_ge(s_bmod, 16)
            for i in range(MT):
                k, col = mod_tile(i)
                dve.wait_ge(s_m[i % 4], 16 * (i // 4 + 1))
                acc = rows[:, col:col + 2 * D]
                nc.vector.scalar_tensor_tensor(out=acc, in0=m_ring[:, i % 4, :], scalar=siluc[:, k:k + 1],
                                               in1=acc, op0=ALU.mult, op1=ALU.add).then_inc(s_mu, 1)
                dve.drain()

            dve.wait_ge(s_gs, 1)
            nc.vector.scalar_tensor_tensor(out=gx0, in0=gx0, scalar=0.0, in1=gx1, op0=ALU.min, op1=ALU.subtract)
            dve.drain()
            for i in range(GP):
                last = nc.vector.tensor_tensor_scan(gx1[:, SEQ * i:SEQ * (i + 1)], restart,
                                                    gx0[:, SEQ * i:SEQ * (i + 1)], 0.0, ALU.mult, ALU.add)
            last.then_inc(s_gv, 1)
            dve.drain()
            bch = gx1.rearrange("p (n t) -> p n t", t=CHUNK)
            nc.vector.tensor_tensor(gx2.rearrange("p (n t) -> p n t", t=CHUNK),
                                    bch[:, :, CHUNK - 1:CHUNK].to_broadcast((P, GP * NCH, CHUNK)),
                                    bch, ALU.subtract).then_inc(s_gv, 1)
            nc.vector.memset(attn.rearrange("p i b t -> p (i b t)"), 0.0)
            dve.wait_ge(s_gs, 2)
            qf, kf = mid[:, 0:1024], mid[:, 1024:2048]
            nc.vector.scalar_tensor_tensor(out=qf, in0=qf, scalar=float(DK) ** -0.5, in1=gx0,
                                           op0=ALU.mult, op1=ALU.mult)
            dve.wait_ge(s_gs, 3)
            nc.vector.tensor_tensor(gx2, kf, gx2, ALU.mult).then_inc(s_gv, 1)
            dve.wait_ge(s_gs, 4)
            dve.drain()
            nc.vector.tensor_tensor(kf, kf, gx1, ALU.mult).then_inc(s_gv, 1)

            def conv_job(j):
                _, kind, i, _, lo, hi = jobs[j]
                dve.wait_ge(s_job, j + 1)
                src = bank[job_bank[j]][:, 0:hi - lo]
                if kind == "ch":
                    at_cc = next(m for m, job in enumerate(jobs) if job[1:3] == ("cc", i) and job[4] == lo)
                    dve.wait_ge(s_ja, read_by[at_cc][1])
                    nc.vector.tensor_tensor(uconv[:, i, lo:hi], src, cgate[:, i, lo:hi], ALU.mult).then_inc(s_jv, 1)
                    return
                y = mixT[:, i, :]
                tap = [pcol[:, 14 + CC * t + i:15 + CC * t + i] for t in range(3)]
                dve.drain()
                nc.vector.tensor_scalar(y[:, lo:hi], uconv[:, i, lo:hi], tap[2], None, ALU.mult)
                dve.drain()
                for back in (1, 2):
                    at = max(lo, back)
                    nc.vector.scalar_tensor_tensor(out=y[:, at:hi], in0=uconv[:, i, at - back:hi - back],
                                                   scalar=tap[2 - back], in1=y[:, at:hi],
                                                   op0=ALU.mult, op1=ALU.add)
                    dve.drain()
                nc.vector.tensor_tensor(y[:, lo:hi], y[:, lo:hi], src, ALU.mult).then_inc(s_jv, 1)

            ebt = gx0.rearrange("p (c t) -> p c t", c=GP)

            def states(i):
                dve.wait_ge(s_kv, i + 1)
                kv = pb[:, :].rearrange("p (o n e) -> p n o e", o=2, e=P)
                nc.vector.tensor_copy(state[i][:, 0, :], kv[:, 0, 0, :])
                dve.drain()
                for n in range(1, NCH - 1):
                    last = nc.vector.scalar_tensor_tensor(
                        out=state[i][:, n, :], in0=state[i][:, n - 1, :],
                        scalar=ebt[:, i, CHUNK * n + CHUNK - 1:CHUNK * (n + 1)], in1=kv[:, n // 2, n % 2, :],
                        op0=ALU.mult, op1=ALU.add)
                    dve.drain() if n < NCH - 2 else last.then_inc(s_st, 1)

            def mask(hd):
                dve.wait_ge(s_at, hd + 1)
                if hd >= 2:
                    dve.wait_ge(s_o, hd - 1)
                keep = causal[:, :].bitcast(U32).unsqueeze(1).to_broadcast((P, NB, P))
                nc.vector.copy_predicated(attn[:, hd % 2], keep,
                                          bank[6 + hd % 2].rearrange("p (b t) -> p b t", b=NB)).then_inc(s_am, 1)

            def normalise(hd):
                dve.wait_ge(s_ms, hd + 1)
                nc.vector.tensor_scalar(rms[:, hd % 2, :], bank[2 + hd % 2], 1.0 / P, RMS_EPS,
                                        ALU.mult, ALU.add).then_inc(s_msv, 1)
                dve.wait_ge(s_rt, hd + 1)
                nc.vector.reciprocal(rms[:, hd % 2, :], rms[:, hd % 2, :])
                dve.drain()
                y = mixT[:, CC + hd, :]
                nc.vector.tensor_tensor(y, bank[4 + hd % 2], rms[:, hd % 2, :], ALU.mult)
                dve.drain()
                nc.vector.scalar_tensor_tensor(out=y, in0=y, scalar=pcol[:, 10 + hd:11 + hd], in1=r_[:, hd, :],
                                               op0=ALU.mult, op1=ALU.mult).then_inc(s_mix, 1)

            conv = n_attn
            states(0)
            conv_job(conv + 2)
            states(1)
            mask(0)
            mask(1)
            conv_job(conv + 3)
            mask(2)
            conv_job(conv + 4)
            conv_job(conv + 5)
            mask(3)
            normalise(0)
            normalise(1)
            conv_job(conv + 8)
            dve.wait_ge(s_fold, 1)
            normalise(2)
            conv_job(conv + 9)
            normalise(3)
            conv_job(conv + 10)
            conv_job(conv + 11)

            def standardise(n, ln_t, dst):
                for i in range(2):
                    nc.vector.bn_stats(stats[:, i, :], ln_t[:, 512 * i:512 * (i + 1)])
                dve.drain()
                nc.vector.bn_aggr(mv, stats)
                dve.drain()
                nc.vector.tensor_scalar(mv[:, 1:2], mv[:, 1:2], LN_EPS, None, ALU.add).then_inc(s_lv, 1)
                dve.wait_ge(s_ls, n)
                nc.vector.reciprocal(rstd, std)
                dve.drain()
                nc.vector.tensor_scalar(dst, ln_t, mv[:, 0:1], rstd, ALU.subtract, ALU.mult)
                dve.drain()

            def add_x(b):
                dve.wait_ge(s_wop, b + 1)
                nc.vector.scalar_tensor_tensor(out=ln_ts[b % 2], in0=x_sb[:, b, :], scalar=ALPHA,
                                               in1=mix_ps(b)[:, :],
                                               op0=ALU.mult, op1=ALU.add).then_inc(s_lnz, 1)
                dve.drain()

            def front(b):
                standardise(b + 1, ln_ts[b % 2], x_sb[:, b, :])
                nc.vector.tensor_tensor(h2[:, b, :], x_sb[:, b, :], scale2, ALU.mult)
                dve.drain()
                nc.vector.tensor_tensor(h2[:, b, :], h2[:, b, :], shift2, ALU.add).then_inc(s_h2, 1)
                dve.drain()

            def top16(values, best_, where, rest_):
                nc.vector.max(best_[:, 0:8], values)
                dve.drain()
                nc.vector.max_index(where[:, 0:8], best_[:, 0:8], values)
                last = nc.vector.match_replace(out=rest_, in_to_replace=best_[:, 0:8], in_values=values,
                                               imm_value=LOWEST)
                dve.drain()
                nc.vector.max(best_[:, 8:16], rest_)
                dve.drain()
                nc.vector.max_index(where[:, 8:16], best_[:, 8:16], rest_)
                return last

            def select(g, b):
                par = b % 2
                dve.wait_ge(s_sc, g + 1)
                dve.nop(nofuse=True)
                for p in range(2):
                    last = top16(sps[par][:, p, :], best[:, p, :], besti[:, p, :], rest[:, p, :])
                last.then_inc(s_scr, 1)
                dve.drain()
                nc.vector.tensor_tensor(cand, best[:, 0, :].unsqueeze(2).to_broadcast((P, TOPK, TOPK)),
                                        best[:, 1, :].unsqueeze(1).to_broadcast((P, TOPK, TOPK)), ALU.add)
                nc.vector.tensor_copy(bestf, besti)
                dve.drain()
                top16(cand.rearrange("p a b -> p (a b)"), top[:, par, :], pos, cand2.rearrange("p a b -> p (a b)"))
                nc.vector.tensor_scalar(ntop[:, par, :], top[:, par, 0:1], -1.0, None, ALU.mult).then_inc(s_top, 1)
                dve.drain()
                nc.vector.tensor_scalar(part[:, :, 0], pos, 4, None, ALU.logical_shift_right)
                nc.vector.tensor_scalar(part[:, :, 1], pos, TOPK - 1, None, ALU.bitwise_and)
                dve.drain()
                nc.vector.tensor_copy(partf, part)
                dve.drain()
                whole = (P, TOPK, 2, TOPK)
                nc.vector.tensor_tensor(pick, seq16[:, :].unsqueeze(1).unsqueeze(1).to_broadcast(whole),
                                        partf.unsqueeze(3).to_broadcast(whole), ALU.is_equal)
                dve.drain()
                nc.vector.tensor_tensor(pick, pick, bestf.unsqueeze(1).to_broadcast(whole), ALU.mult)
                dve.drain()
                nc.vector.tensor_reduce(keys, pick, mybir.AxisListType.X, ALU.add)
                dve.drain()
                nc.vector.scalar_tensor_tensor(out=idx[:, b, :], in0=keys[:, :, 0], scalar=float(NKEYS),
                                               in1=keys[:, :, 1], op0=ALU.mult, op1=ALU.add).then_inc(s_idx, 1)
                dve.drain()

            def add_y(g, b, into_new):
                dve.wait_ge(s_vu, 16 * g + 16)
                y = yps[b % 2][:, :]
                if into_new:
                    nc.vector.tensor_copy(yacc[:, b, :], y).then_inc(s_yr, 1)
                else:
                    nc.vector.tensor_tensor(yacc[:, b, :], yacc[:, b, :], y, ALU.add).then_inc(s_yr, 1)

            def dot(b, g, s):
                dve.wait_ge(s_u[s % RING], 16 * (2 * g + s // RING + 1))
                row = u_ring[:, s % RING, :]
                nc.vector.tensor_tensor_reduce(out=row, in0=row, in1=h2[:, b, :], scale=1.0, scalar=0.0,
                                               op0=ALU.mult, op1=ALU.add,
                                               accum_out=dots[:, b % 2, s:s + 1]).then_inc(s_dot, 1)

            def weights(b, g):
                dve.wait_ge(s_exp, g + 1)
                nc.vector.reciprocal(rsum, esum[:, b % 2, :])
                dve.drain()
                dve.wait_ge(s_gel, g + 1)
                nc.vector.scalar_tensor_tensor(out=coef[:, b % 2, :], in0=act_[:, b % 2, :], scalar=rsum,
                                               in1=expo[:, b % 2, :], op0=ALU.mult, op1=ALU.mult).then_inc(s_coef, 1)

            def slot(h, b, g, more=True):
                if more:
                    select(g + 1, (b + 1) % NB)
                for s in range(TOPK):
                    dot(b, g, s)
                weights(b, g)

            def prepare(b):
                dve.wait_ge(s_x1, b + 1)
                dve.drain()
                nc.vector.tensor_tensor(ln_ts[b % 2], yacc[:, b, :], gate2, ALU.mult)
                dve.drain()
                nc.vector.scalar_tensor_tensor(out=ln_ts[b % 2], in0=x_sb[:, b, :], scalar=ALPHA, in1=ln_ts[b % 2],
                                               op0=ALU.mult, op1=ALU.add)

            def finish(g, b):
                ln_t = ln_ts[b % 2]
                dve.wait_ge(s_vu, 16 * g + 16)
                nc.vector.tensor_tensor(yacc[:, b, :], yps[b % 2][:, :], gate2, ALU.mult).then_inc(s_yr, 1)
                dve.drain()
                nc.vector.tensor_tensor(ln_t, ln_t, yacc[:, b, :], ALU.add)
                dve.drain()
                standardise(NB + b + 1, ln_t, ln_t)
                for half in range(2):
                    cols = slice(D // 2 * half, D // 2 * (half + 1))
                    nc.vector.tensor_tensor(ln_t[:, cols], ln_t[:, cols], ln2g[:, cols], ALU.mult)
                    dve.drain()
                    nc.vector.tensor_tensor(x_sb[:, b, cols], ln_t[:, cols], ln2b[:, cols], ALU.add).then_inc(s_fin, 1)

            add_x(0)
            front(0)
            conv_job(n_first)
            conv_job(n_first + 1)
            select(0, 0)
            conv_job(n_first + 4)
            conv_job(n_first + 5)
            for s in range(RING // 2):
                dot(0, 0, s)
            add_x(1)
            front(1)
            conv_job(n_first + 6)
            conv_job(n_first + 7)
            for s in range(RING // 2, RING):
                dot(0, 0, s)
            select(1, 1)
            for s in range(RING, TOPK):
                dot(0, 0, s)
            weights(0, 0)
            for s in range(RING // 2):
                dot(1, 1, s)
            add_x(2)
            front(2)
            add_x(3)
            for s in range(RING // 2, RING):
                dot(1, 1, s)
            front(3)
            select(2, 2)
            for s in range(RING, TOPK):
                dot(1, 1, s)
            weights(1, 1)
            add_y(0, 0, True)
            for b in range(2, NB):
                slot(0, b, b)
                add_y(b - 1, b - 1, True)
            nc.vector.memset(yacc[:, NB - 1, :], 0.0)
            dve.drain()
            with dve.Fori(1, HEADS - 1) as h:
                for b in range(NB):
                    g = h * NB + b
                    slot(h, b, g)
                    add_y(g - 1, (b - 1) % NB, False)
            dve.wait_ge(s_ln2r, 32)
            dve.wait_ge(s_rbe, 8)
            for b in range(NB):
                g = NG - NB + b
                slot(HEADS - 1, b, g, more=b < NB - 1)
                if b == 0:
                    add_y(g - 1, NB - 1, False)
                else:
                    prepare(b - 1)
                    finish(g - 1, b - 1)
            prepare(NB - 1)
            finish(NG - 1, NB - 1)

        @block.tensor
        def _(pe):
            pe.wait_ge(s_const, 1)
            pe.wait_ge(s_par, 64)
            nc.tensor.transpose(bank[6][:, 0:26], prow[0:26, :], ident[0:26, 0:26]).then_inc(s_colps, 1)
            pe.wait_ge(s_x, 16)
            for k in range(KC):
                if k >= 2:
                    pe.wait_ge(s_xte, k - 1)
                for b in range(NB):
                    mm = nc.tensor.transpose(bank[4 + k % 2][:, b * P:(b + 1) * P], x_sb[:, b, k * P:(k + 1) * P],
                                             ident[:, :])
                mm.then_inc(s_xt, 1)
            pe.wait_ge(s_mu, KC)
            for part in range(2):
                for k in range(KC * part // 2, KC * (part + 1) // 2):
                    for j in (k, KC + k):
                        mm = nc.tensor.matmul(bank[7 - part][:, j:j + 1], mod_cols[:, j * P:(j + 1) * P],
                                              ones[:, 0:1], start=True, stop=True)
                mm.then_inc(s_mc, 1)

            def mod_rows(steps):
                pe.wait_ge(s_mu, MT)
                for j in steps:
                    if j >= 2:
                        pe.wait_ge(s_rbe, j - 1)
                    nc.tensor.matmul(rows_bank(j), ones[:, :], rows[:, 2 * D + 512 * j:2 * D + 512 * (j + 1)],
                                     start=True, stop=True).then_inc(s_rb, 1)

            def gates():
                pe.wait_ge(s_wq, 16)
                pe.wait_ge(s_ja, 1)
                for i in range(GP):
                    nc.tensor.matmul(bank[4 + i], gate_up[:, i * P:(i + 1) * P], glr, start=True,
                                     stop=True).then_inc(s_z, 1)

            def project(j):
                n, kind, i, part, first, last = jobs[j]
                if j == first_job[n]:
                    pe.wait_ge(s_w[w_slot(n)], 16 * (n // 4 + 1))
                if before[j] is not None:
                    e, count = read_by[before[j]]
                    pe.wait_ge(s_ja if e == "a" else s_jv, count)
                w, to = w_ring[:, w_slot(n)], bank[job_bank[j]]
                if kind == "v":
                    for bb in range(2):
                        b = 2 * i[1] + bb
                        for k in range(KC):
                            mm = nc.tensor.matmul(to[:, WT * bb:WT * (bb + 1)], hT[:, k, b * P:(b + 1) * P],
                                                  w[:, k, :], start=k == 0, stop=k == KC - 1)
                else:
                    m = RANK if kind == "glr" else P
                    lo = P * part
                    for k in range(KC):
                        if j == 0:
                            pe.wait_ge(s_h, k + 1)
                        mm = nc.tensor.matmul(to[0:m, 0:last - first], w[:, k, lo:lo + m], hT[:, k, first:last],
                                              start=k == 0, stop=k == KC - 1)
                mm.then_inc(s_job, 1)

            def turn_keys():
                pe.wait_ge(s_gv, 3)
                kl = gx2.rearrange("p (c t) -> p c t", c=GP)
                for i in range(GP):
                    for b in range(NB):
                        mm = nc.tensor.transpose(bank[4 + i][:, b * P:(b + 1) * P], kl[:, i, b * P:(b + 1) * P],
                                                 ident[:, :])
                    mm.then_inc(s_klp, 1)

            def chunk_kv(i):
                pe.wait_ge(s_klt, i + 1)
                if i == 0:
                    for j in range(n_attn):
                        if job_bank[j] in (2, 3) and j + 4 >= n_attn:
                            pe.wait_ge(s_ja, read_by[j][1])
                else:
                    pe.wait_ge(s_st, i)
                for n in range(NCH - 1):
                    lo = CHUNK * (n % 2)
                    for hh in range(2):
                        hd = 2 * i + hh
                        col = 512 * (n % 2) + P * (n // 2)
                        mm = nc.tensor.matmul(pb[DK * hh:DK * (hh + 1), col:col + P],
                                              klT[lo:lo + CHUNK, i, n // 2, DK * hh:DK * (hh + 1)],
                                              v_[lo:lo + CHUNK, n // 2, hd * P:(hd + 1) * P], start=True, stop=True)
                mm.then_inc(s_kv, 1)

            def scores_of(hd):
                i, lo = hd // 2, DK * (hd % 2)
                if hd >= 2:
                    pe.wait_ge(s_am, hd - 1)
                for b in range(NB):
                    mm = nc.tensor.matmul(bank[6 + hd % 2][:, b * P:(b + 1) * P],
                                          k_[lo:lo + DK, i, b * P:(b + 1) * P],
                                          q_[lo:lo + DK, i, b * P:(b + 1) * P], start=True, stop=True)
                mm.then_inc(s_at, 1)

            def outputs_of(hd):
                i, lo = hd // 2, DK * (hd % 2)
                pe.wait_ge(s_am, hd + 1)
                pe.wait_ge(s_st, i + 1)
                if hd >= 2:
                    pe.wait_ge(s_mix, hd - 1)
                o = bank[4 + hd % 2]
                for b in range(NB):
                    mm = nc.tensor.matmul(o[:, b * P:(b + 1) * P], v_[:, b, hd * P:(hd + 1) * P],
                                          attn[:, hd % 2, b, :], start=True, stop=False, skip_group_check=True)
                    for n in (2 * b, 2 * b + 1):
                        if n == 0:
                            continue
                        mm = nc.tensor.matmul(o[:, n * CHUNK:(n + 1) * CHUNK], state[i][lo:lo + DK, n - 1, :],
                                              q_[lo:lo + DK, i, n * CHUNK:(n + 1) * CHUNK],
                                              start=False, stop=n % 2 == 1, skip_group_check=True)
                mm.then_inc(s_o, 1)

            def mean_square(hd):
                pe.wait_ge(s_sq, hd + 1)
                if hd < 2:
                    pe.wait_ge(s_st, GP)
                else:
                    pe.wait_ge(s_msv, hd - 1)
                nc.tensor.matmul(bank[2 + hd % 2], ones[:, :], sq[:, hd % 2, :], start=True, stop=True).then_inc(s_ms, 1)

            for j in range(n_attn):
                project(j)
                if j == 2:
                    gates()
            mod_rows(range(6))
            conv = n_attn
            project(conv)
            turn_keys()
            project(conv + 1)
            chunk_kv(0)
            project(conv + 2)
            chunk_kv(1)
            pe.wait_ge(s_gv, 4)
            pe.wait_ge(s_rbe, 6)
            scores_of(0)
            scores_of(1)
            project(conv + 3)
            outputs_of(0)
            scores_of(2)
            project(conv + 4)
            project(conv + 5)
            outputs_of(1)
            mean_square(0)
            scores_of(3)
            project(conv + 6)
            project(conv + 7)
            mean_square(1)
            outputs_of(2)
            project(conv + 8)
            mean_square(2)
            outputs_of(3)
            project(conv + 9)
            mean_square(3)
            project(conv + 10)
            project(conv + 11)

            def scores(g, b):
                if not (isinstance(g, int) and g < 2):
                    pe.wait_ge(s_scr, g - 1)
                for p in range(2):
                    mm = nc.tensor.matmul(sps[b % 2][:, p, :], qT[:, p, b * P:(b + 1) * P], skT[:, p, :],
                                          start=True, stop=True)
                mm.then_inc(s_sc, 1)

            def subkeys(h):
                pe.wait_ge(s_wq, 16 * (2 * h + 3))
                for p in range(2):
                    mm = nc.tensor.transpose(pc[:, NKEYS * p:NKEYS * (p + 1)], sk_sb[:, p, :], ident[:, :])
                mm.then_inc(s_skp, 1)

            def mix(b):
                if b == 1:
                    pe.wait_ge(s_ja, read_by[n_first + 3][1])
                elif b == 2:
                    pe.wait_ge(s_jv, counts["v"])
                elif b == 3:
                    pe.wait_ge(s_lnz, 2)
                for half in range(2):
                    for n, k in enumerate([CC, CC + 1, CC + 2, 0, 1, CC + 3, 2, 3]):
                        if b == 0 and half == 0:
                            if n == 0:
                                pe.wait_ge(s_mix, GH - 1)
                            if k == 0:
                                pe.wait_ge(s_jv, read_by[conv + 5][1])
                            if k == CC + 3:
                                pe.wait_ge(s_mix, GH)
                            if k == 2:
                                pe.wait_ge(s_jv, read_by[conv + 11][1])
                            pe.wait_ge(s_wg, k + 1)
                        mm = nc.tensor.matmul(mix_ps(b)[:, 512 * half:512 * (half + 1)], mixT[:, k, b * P:(b + 1) * P],
                                              wout[:, k, 512 * half:512 * (half + 1)], start=n == 0, stop=n == KC - 1)
                mm.then_inc(s_wop, 1)

            def turn(b):
                pe.wait_ge(s_h2, b + 1)
                if b > 0:
                    pe.wait_ge(s_qe, b)
                for k in range(KC):
                    mm = nc.tensor.transpose(pc[:, k * P:(k + 1) * P], h2[:, b, k * P:(k + 1) * P], ident[:, :])
                mm.then_inc(s_tp, 1)

            def query(b):
                pe.wait_ge(s_tpe, b + 1)
                for p in range(2):
                    for k in range(KC):
                        mm = nc.tensor.matmul(pc[:, 512 * p:512 * p + P], wq_sb[:, k, p * P:(p + 1) * P],
                                              hT[:, k, b * P:(b + 1) * P], start=k == 0, stop=k == KC - 1)
                mm.then_inc(s_qp, 1)

            def first_scores(b):
                pe.wait_ge(s_qe, b + 1)
                scores(b, b)

            def front(b):
                turn(b)
                query(b)
                first_scores(b)

            def next_query(h, p):
                if p == 0:
                    pe.wait_ge(s_wq, 16 * (2 * h + 3))
                    pe.wait_ge(s_ske, h)
                for k in range(KC):
                    mm = nc.tensor.matmul(pc[:, 512 * p:512 * (p + 1)], wq_sb[:, k, p * P:(p + 1) * P],
                                          hT[:, k, :], start=k == 0, stop=k == KC - 1)
                if p == 1:
                    mm.then_inc(s_qp, 1)
                    pe.wait_ge(s_qe, NB + h)
                    subkeys(h)

            def weigh(g, b, experts=range(TOPK)):
                if not (isinstance(g, int) and g < 2):
                    pe.wait_ge(s_yr, g - 1)
                for s in experts:
                    pe.wait_ge(s_diag, 16 * g + s + 1)
                    pe.wait_ge(s_v[s % RING], 16 * (2 * g + s // RING + 1))
                    for half in range(2):
                        mm = nc.tensor.matmul(yps[b % 2][:, 512 * half:512 * (half + 1)], diag[:, s, :],
                                              v_ring[:, s % RING, 512 * half:512 * (half + 1)],
                                              start=s == 0, stop=s == TOPK - 1)
                    mm.then_inc(s_vu, 1)

            mix(0)
            subkeys(0)
            project(n_first)
            project(n_first + 1)
            pe.wait_ge(s_ske, 1)
            turn(0)
            pe.wait_ge(s_lnz, 1)
            project(n_first + 2)
            query(0)
            project(n_first + 3)
            first_scores(0)
            project(n_first + 4)
            project(n_first + 5)
            mix(1)
            project(n_first + 6)
            project(n_first + 7)
            front(1)
            mix(2)
            mix(3)
            front(2)
            pe.wait_ge(s_lnz, NB)
            weigh(0, 0, range(RING))
            front(3)
            mod_rows(range(6, 8))
            weigh(0, 0, range(RING, TOPK))
            weigh(1, 1, range(RING))
            pe.wait_ge(s_rbe, 8)
            next_query(1, 0)
            next_query(1, 1)
            pe.wait_ge(s_ske, 2)
            scores(NB, 0)
            weigh(1, 1, range(RING, TOPK))
            scores(NB + 1, 1)
            weigh(2, 2)
            with pe.Fori(1, HEADS - 1) as h:
                for b in range(NB):
                    g = h * NB + b
                    if b == 2:
                        pe.wait_ge(s_ske, h + 2)
                    scores(g + 2, (b + 2) % NB)
                    weigh(g - 1, (b - 1) % NB)
                    if b < 2:
                        next_query(h + 1, b)
            for b in range(NB):
                g = NG - NB + b
                if b < 2:
                    scores(g + 2, b + 2)
                weigh(g - 1, (b - 1) % NB)
            weigh(NG - 1, NB - 1)


_INS = ["x", "c", "w_mod", "b_mod", "w_in", "conv_w", "gla_gate_up", "gla_gate_bias", "gla_norm_g", "w_out",
        "ln1_g", "ln1_b", "peer_wq", "peer_subkeys", "peer_u", "peer_v", "ln2_g", "ln2_b"]


def kernel(**inputs):
    import numpy as np
    import concourse.bacc as bacc
    from concourse.bass_utils import run_bass_kernel_spmd

    nc = bacc.Bacc("TRN2", target_bir_lowering=False, num_devices=1)
    arrays, args = {}, []
    for name in _INS:
        a = np.ascontiguousarray(inputs[name])
        arrays[f"in_{name}"] = a
        args.append(nc.dram_tensor(f"in_{name}", a.shape, mybir.dt.from_np(a.dtype), kind="ExternalInput").ap())
    args.append(nc.dram_tensor("out_0", inputs["x"].shape, F32, kind="ExternalOutput").ap())
    build(nc, *args)
    r = run_bass_kernel_spmd(nc, [arrays], core_ids=[0])
    return r.results[0]["out_0"]
```
